# Optimizing a Trainium2 kernel written in Bass

```python
import jax, jax.numpy as jnp
from jax import lax
import numpy as np

D_MODEL = 1024
BATCH = 1
SEQ = 512
DEPTH = 1

GRID_W = 64
CTX_LEN = 256
DN_HEADS = 8
DN_HEAD_DIM = 128
DN_WIDTH = DN_HEADS * DN_HEAD_DIM
SHORT_CONV = 5
CHUNK = 64
POOL_GROUPS = 4
POOL_WINDOWS = (2, 4, 8, 16)
POOL_WIDTH = D_MODEL
POOL_GROUP_DIM = POOL_WIDTH // POOL_GROUPS
D_MIX = DN_WIDTH + POOL_WIDTH
PROJ_SIZES = (3 * DN_WIDTH, 4 * DN_HEADS, DN_WIDTH, POOL_WIDTH, POOL_WIDTH)
D_PROJ = sum(PROJ_SIZES)
PROJ_SPLITS = tuple(int(s) for s in np.cumsum(PROJ_SIZES)[:-1])
EPS = 1e-6


def _rms_norm(h, gain):
    hf = h.astype(jnp.float32)
    hf = hf * lax.rsqrt(jnp.mean(hf * hf, axis=-1, keepdims=True) + EPS)
    return hf.astype(h.dtype) * gain

def _l2_norm(h):
    hf = h.astype(jnp.float32)
    hf = hf * lax.rsqrt(jnp.sum(hf * hf, axis=-1, keepdims=True) + EPS)
    return hf.astype(h.dtype)

def _short_conv(u, w):
    k = w.shape[0]
    return lax.conv_general_dilated(
        u, w[:, None, :], window_strides=(1,), padding=[(k // 2, k // 2)],
        dimension_numbers=('NWC', 'WIO', 'NWC'), feature_group_count=u.shape[-1])

def _gated_delta_rule(q, k, v, g, beta, s0):
    out_dtype = v.dtype
    q, k, v, g, beta = (t.astype(jnp.float32) for t in (q, k, v, g, beta))
    bsz, nh, length, dk = q.shape
    dv = v.shape[-1]
    n = length // CHUNK
    q = q * dk ** -0.5
    q, k, v = (t.reshape(bsz, nh, n, CHUNK, -1) for t in (q, k, v))
    g = jnp.cumsum(g.reshape(bsz, nh, n, CHUNK), axis=-1)
    beta = beta.reshape(bsz, nh, n, CHUNK, 1)
    incl = jnp.tril(jnp.ones((CHUNK, CHUNK), bool))
    strict = jnp.tril(jnp.ones((CHUNK, CHUNK), bool), -1)
    decay = jnp.exp(jnp.where(incl, g[..., :, None] - g[..., None, :], -jnp.inf))
    kb = k * beta
    a_mat = jnp.where(strict, jnp.einsum('bhncd,bhnsd->bhncs', kb, k) * decay, 0.0)
    eye = jnp.eye(CHUNK, dtype=jnp.float32)
    rhs = jnp.concatenate([v * beta, kb * jnp.exp(g)[..., None]], axis=-1)
    sol = lax.linalg.triangular_solve(eye + a_mat, rhs, left_side=True, lower=True,
                                      unit_diagonal=True)
    u_c, w_c = sol[..., :dv], sol[..., dv:]
    qk = jnp.einsum('bhncd,bhnsd->bhncs', q, k) * decay
    q_dec = q * jnp.exp(g)[..., None]
    g_last = g[..., -1]
    k_tail = k * jnp.exp(g_last[..., None] - g)[..., None]
    xs = tuple(jnp.moveaxis(t, 2, 0) for t in (u_c, w_c, qk, q_dec, k_tail, g_last))

    def step(state, inp):
        u_i, w_i, qk_i, q_i, k_i, gl_i = inp
        v_new = u_i - jnp.einsum('bhcd,bhdv->bhcv', w_i, state)
        o_i = (jnp.einsum('bhcd,bhdv->bhcv', q_i, state)
               + jnp.einsum('bhcs,bhsv->bhcv', qk_i, v_new))
        state = state * jnp.exp(gl_i)[..., None, None] + jnp.einsum('bhcd,bhcv->bhdv', k_i, v_new)
        return state, o_i

    s_final, o = lax.scan(step, s0.astype(jnp.float32), xs)
    o = jnp.moveaxis(o, 0, 2).reshape(bsz, nh, length, dv)
    return o.astype(out_dtype), s_final

def _window_bounds(n, w):
    idx = jnp.arange(n)
    lo = jnp.clip(idx - w // 2, 0, n)
    hi = jnp.clip(idx - w // 2 + w, 0, n)
    return lo, hi

def _pool_grid(u, w):
    bsz, length, ch = u.shape
    rows = length // GRID_W
    grid = u.reshape(bsz, rows, GRID_W, ch)
    sat = jnp.pad(jnp.cumsum(jnp.cumsum(grid, axis=1), axis=2), ((0, 0), (1, 0), (1, 0), (0, 0)))
    lr, hr = _window_bounds(rows, w)
    lc, hc = _window_bounds(GRID_W, w)
    s_hr, s_lr = sat[:, hr], sat[:, lr]
    box = s_hr[:, :, hc] - s_lr[:, :, hc] - s_hr[:, :, lc] + s_lr[:, :, lc]
    cnt = ((hr - lr)[:, None] * (hc - lc)[None, :]).astype(u.dtype)
    return (box / cnt[None, :, :, None]).reshape(bsz, length, ch)

def _pool_seq(u, w):
    length = u.shape[1]
    cs = jnp.pad(jnp.cumsum(u, axis=1), ((0, 0), (1, 0), (0, 0)))
    lo, hi = _window_bounds(length, w)
    return (cs[:, hi] - cs[:, lo]) / (hi - lo).astype(u.dtype)[None, :, None]

def _pool_mixer(u, grid, pool_w, pool_scale):
    bsz, length, _ = u.shape
    pool = _pool_grid if grid else _pool_seq
    groups = jnp.split(u.astype(jnp.float32), POOL_GROUPS, axis=-1)
    d = jnp.stack([pool(gu, w) - gu for gu, w in zip(groups, POOL_WINDOWS)], axis=2)
    y = jnp.einsum('blgc,gce->blge', d.astype(u.dtype), pool_w).reshape(bsz, length, POOL_WIDTH)
    return y * pool_scale

def _mix(h, shift, scale, grid, s0_f, s0_b, gain, w_in, conv_w, a_log, dt_bias, dn_gain,
         pool_w, pool_scale):
    bsz, length, _ = h.shape
    hn = _rms_norm(h, gain) * (1 + scale) + shift
    proj = jnp.einsum('bld,dp->blp', hn, w_in)
    qkv, ab, z_dn, u_pool, z_pool = jnp.split(proj, PROJ_SPLITS, axis=-1)
    qkv = jax.nn.silu(_short_conv(qkv, conv_w))
    q, k, v = (t.reshape(bsz, length, DN_HEADS, DN_HEAD_DIM).transpose(0, 2, 1, 3)
               for t in jnp.split(qkv, 3, axis=-1))
    q, k = _l2_norm(q), _l2_norm(k)
    ab = ab.astype(jnp.float32).reshape(bsz, length, 2, 2, DN_HEADS).transpose(2, 3, 0, 4, 1)
    g = -jnp.exp(a_log.astype(jnp.float32))[:, None, :, None] * jax.nn.softplus(
        ab[0] + dt_bias.astype(jnp.float32)[:, None, :, None])
    beta = jax.nn.sigmoid(ab[1])
    o_f, s_f = _gated_delta_rule(q, k, v, g[0], beta[0], s0_f)
    o_b, s_b = _gated_delta_rule(jnp.flip(q, 2), jnp.flip(k, 2), jnp.flip(v, 2),
                                 jnp.flip(g[1], -1), jnp.flip(beta[1], -1), s0_b)
    o = _rms_norm(o_f + jnp.flip(o_b, 2), dn_gain)
    o = o.transpose(0, 2, 1, 3).reshape(bsz, length, DN_WIDTH) * jax.nn.silu(z_dn)
    y_pool = _pool_mixer(u_pool, grid, pool_w, pool_scale) * jax.nn.silu(z_pool)
    return jnp.concatenate([o, y_pool], axis=-1), s_f, s_b

def first_inputs(seed: int = 0) -> dict:
    key = jax.random.key(seed)
    ks = jax.random.split(key, 20)
    f32 = jnp.float32
    nrm = lambda k, shape, s: jax.random.normal(k, shape, f32) * s
    a_init = jnp.log(jax.random.uniform(ks[10], (DEPTH, 2, DN_HEADS), f32, 1.0, 16.0))
    dt = jnp.exp(jax.random.uniform(ks[11], (DEPTH, 2, DN_HEADS), f32,
                                    float(np.log(1e-3)), float(np.log(1e-1))))
    dt_bias = dt + jnp.log(-jnp.expm1(-dt))
    return {
        "x": nrm(ks[0], (BATCH, SEQ, D_MODEL), 1.0),
        "c": nrm(ks[1], (BATCH, D_MODEL), 1.0),
        "ctx": nrm(ks[2], (BATCH, CTX_LEN, D_MODEL), 1.0),
        "c_ctx": nrm(ks[3], (D_MODEL,), 1.0),
        "w_mod": nrm(ks[4], (DEPTH, D_MODEL, 3 * D_MODEL), D_MODEL ** -0.5),
        "b_mod": nrm(ks[5], (DEPTH, 3 * D_MODEL), 0.01),
        "norm_gain": 1.0 + nrm(ks[6], (DEPTH, D_MODEL), 0.1),
        "w_in": nrm(ks[7], (DEPTH, D_MODEL, D_PROJ), D_MODEL ** -0.5),
        "conv_w": nrm(ks[8], (DEPTH, SHORT_CONV, 3 * DN_WIDTH), SHORT_CONV ** -0.5),
        "a_log": a_init,
        "dt_bias": dt_bias,
        "dn_norm_gain": 1.0 + nrm(ks[12], (DEPTH, DN_HEAD_DIM), 0.1),
        "pool_w": nrm(ks[13], (DEPTH, POOL_GROUPS, POOL_GROUP_DIM, POOL_GROUP_DIM),
                       POOL_GROUP_DIM ** -0.5),
        "pool_scale": 1.0 + nrm(ks[14], (DEPTH, POOL_WIDTH), 0.1),
        "w_out": nrm(ks[15], (DEPTH, D_MIX, D_MODEL), D_MIX ** -0.5),
        "final_gain": 1.0 + nrm(ks[16], (D_MODEL,), 0.1),
    }

def first_block(x, c, ctx, c_ctx, w_mod, b_mod, norm_gain, w_in, conv_w, a_log, dt_bias,
              dn_norm_gain, pool_w, pool_scale, w_out, final_gain):
    bsz = x.shape[0]
    silu_c = jax.nn.silu(c)
    silu_cc = jax.nn.silu(c_ctx)
    s_zero = jnp.zeros((bsz, DN_HEADS, DN_HEAD_DIM, DN_HEAD_DIM), jnp.float32)
    for layer in range(DEPTH):
        mod_x = (silu_c @ w_mod[layer] + b_mod[layer])[:, None, :]
        shift_x, scale_x, gate_x = jnp.split(mod_x, 3, axis=-1)
        mod_c = silu_cc @ w_mod[layer] + b_mod[layer]
        shift_c, scale_c, gate_c = jnp.split(mod_c, 3, axis=-1)
        params = (norm_gain[layer], w_in[layer], conv_w[layer], a_log[layer], dt_bias[layer],
                  dn_norm_gain[layer], pool_w[layer], pool_scale[layer])
        y_ctx, s_f, s_b = _mix(ctx, shift_c, scale_c, False, s_zero, s_zero, *params)
        y_x, _, _ = _mix(x, shift_x, scale_x, True, s_f, s_b, *params)
        x = x + gate_x * jnp.einsum('blm,md->bld', y_x, w_out[layer])
        if layer < DEPTH - 1:
            ctx = ctx + gate_c * jnp.einsum('blm,md->bld', y_ctx, w_out[layer])
    return _rms_norm(x, final_gain)


DEPTH_2 = 2

N_HEADS = 8
HEAD_DIM = 64
ATTN_WIDTH = N_HEADS * HEAD_DIM
CONV_CH = 512
CONV_K = 31
D_FF = 2816
D_PLE = 256
Q_BLOCK = 128
FFN_RES = 0.5

Q0 = 0
K0 = Q0 + ATTN_WIDTH
V0 = K0 + ATTN_WIDTH
F0 = V0 + ATTN_WIDTH
C0 = F0 + N_HEADS
GA0 = C0 + 2 * CONV_CH
GC0 = GA0 + D_MODEL
IN_COLS = GC0 + D_MODEL


def rmsnorm(x, g):
    xf = x.astype(jnp.float32)
    y = xf * lax.rsqrt(jnp.mean(xf * xf, axis=-1, keepdims=True) + EPS)
    return (y * g.astype(jnp.float32)).astype(x.dtype)

def swiglu(x, w_in, w_out):
    a, b = jnp.split(x @ w_in, 2, axis=-1)
    return (jax.nn.silu(a) * b) @ w_out

def forgetting_attention(q, k, v, f_logit):
    b, s, h, dh = q.shape
    scale = 1.0 / float(np.sqrt(dh))
    c = jnp.cumsum(jax.nn.log_sigmoid(f_logit.astype(jnp.float32)), axis=1)
    c = jnp.transpose(c, (0, 2, 1))
    qh = jnp.transpose(q, (0, 2, 1, 3))
    kh = jnp.transpose(k, (0, 2, 1, 3))
    vh = jnp.transpose(v, (0, 2, 1, 3))
    outs = []
    for blk in range(s // Q_BLOCK):
        qs, qe = blk * Q_BLOCK, (blk + 1) * Q_BLOCK
        sc = jnp.einsum('bhqd,bhkd->bhqk', qh[:, :, qs:qe], kh[:, :, :qe]).astype(jnp.float32) * scale
        sc = sc + (c[:, :, qs:qe, None] - c[:, :, None, :qe])
        causal = jnp.arange(qs, qe)[:, None] >= jnp.arange(qe)[None, :]
        sc = jnp.where(causal[None, None], sc, -jnp.inf)
        pr = jax.nn.softmax(sc, axis=-1).astype(vh.dtype)
        outs.append(jnp.einsum('bhqk,bhkd->bhqd', pr, vh[:, :, :qe]))
    o = jnp.concatenate(outs, axis=2)
    return jnp.transpose(o, (0, 2, 1, 3)).reshape(b, s, h * dh)

def conformer_conv(glu_in, conv_w, conv_b, g_conv):
    a = glu_in[..., :CONV_CH] * jax.nn.sigmoid(glu_in[..., CONV_CH:])
    y = lax.conv_general_dilated(
        a, conv_w[:, None, :].astype(a.dtype), window_strides=(1,),
        padding=[(CONV_K - 1, 0)], dimension_numbers=('NWC', 'WIO', 'NWC'),
        feature_group_count=CONV_CH) + conv_b
    return jax.nn.silu(rmsnorm(y, g_conv))

def hybrid_mixer(u, w_in, b_f, w_attn_out, conv_w, conv_b, g_conv, w_conv_out, w_out):
    b, s, _ = u.shape
    z = u @ w_in
    q = z[..., Q0:K0].reshape(b, s, N_HEADS, HEAD_DIM)
    k = z[..., K0:V0].reshape(b, s, N_HEADS, HEAD_DIM)
    v = z[..., V0:F0].reshape(b, s, N_HEADS, HEAD_DIM)
    f_logit = z[..., F0:C0] + b_f
    y_attn = forgetting_attention(q, k, v, f_logit) @ w_attn_out
    y_conv = conformer_conv(z[..., C0:GA0], conv_w, conv_b, g_conv) @ w_conv_out
    merged = jax.nn.sigmoid(z[..., GA0:GC0]) * y_attn + jax.nn.sigmoid(z[..., GC0:]) * y_conv
    return merged @ w_out

def second_inputs(seed: int = 0) -> dict:
    key = jax.random.key(seed)
    ks = jax.random.split(key, 24)
    L, D, F = DEPTH_2, D_MODEL, D_FF
    f32 = jnp.float32

    def w(k, shape, fan_in):
        return jax.random.normal(k, shape, f32) * (fan_in ** -0.5)

    def gain(k, shape):
        return 1.0 + 0.05 * jax.random.normal(k, shape, f32)

    return {
        "x": jax.random.normal(ks[0], (BATCH, SEQ, D), f32),
        "p": jax.random.normal(ks[1], (DEPTH_2, BATCH, SEQ, D_PLE), f32),
        "g_ff1": gain(ks[2], (L, D)),
        "w_ff1_in": w(ks[3], (L, D, 2 * F), D),
        "w_ff1_out": w(ks[4], (L, F, D), F),
        "g_mix": gain(ks[5], (L, D)),
        "w_in": w(ks[6], (L, D, IN_COLS), D),
        "b_f": 2.0 + 0.5 * jax.random.normal(ks[7], (L, N_HEADS), f32),
        "w_attn_out": w(ks[8], (L, ATTN_WIDTH, D), ATTN_WIDTH),
        "conv_w": w(ks[9], (L, CONV_K, CONV_CH), CONV_K),
        "conv_b": 0.02 * jax.random.normal(ks[10], (L, CONV_CH), f32),
        "g_conv": gain(ks[11], (L, CONV_CH)),
        "w_conv_out": w(ks[12], (L, CONV_CH, D), CONV_CH),
        "w_out": w(ks[13], (L, D, D), D),
        "g_ff2": gain(ks[14], (L, D)),
        "w_ff2_in": w(ks[15], (L, D, 2 * F), D),
        "w_ff2_out": w(ks[16], (L, F, D), F),
        "g_ple": gain(ks[17], (L, D)),
        "w_ple_gate": w(ks[18], (L, D, D), D),
        "w_ple_proj": w(ks[19], (L, D_PLE, D), D_PLE),
        "g_final": gain(ks[20], (D,)),
    }

def second_block(x, p, g_ff1, w_ff1_in, w_ff1_out, g_mix, w_in, b_f, w_attn_out,
              conv_w, conv_b, g_conv, w_conv_out, w_out, g_ff2, w_ff2_in, w_ff2_out,
              g_ple, w_ple_gate, w_ple_proj, g_final):
    h = x
    for i in range(DEPTH_2):
        h = h + FFN_RES * swiglu(rmsnorm(h, g_ff1[i]), w_ff1_in[i], w_ff1_out[i])
        h = h + hybrid_mixer(rmsnorm(h, g_mix[i]), w_in[i], b_f[i], w_attn_out[i],
                             conv_w[i], conv_b[i], g_conv[i], w_conv_out[i], w_out[i])
        h = h + FFN_RES * swiglu(rmsnorm(h, g_ff2[i]), w_ff2_in[i], w_ff2_out[i])
        gate = jax.nn.sigmoid(rmsnorm(h, g_ple[i]) @ w_ple_gate[i])
        h = h + gate * (p[i] @ w_ple_proj[i])
    return rmsnorm(h, g_final)


def setup_inputs(seed=0):
    out = dict(first_inputs(seed))
    for name, value in second_inputs(seed + 1).items():
        if name != "x":
            out[name + "_2"] = value
    return out


def reference(
    x, c, ctx, c_ctx, w_mod, b_mod, norm_gain, w_in, conv_w, a_log, dt_bias, dn_norm_gain,
    pool_w, pool_scale, w_out, final_gain, p_2, g_ff1_2, w_ff1_in_2, w_ff1_out_2, g_mix_2,
    w_in_2, b_f_2, w_attn_out_2, conv_w_2, conv_b_2, g_conv_2, w_conv_out_2, w_out_2, g_ff2_2,
    w_ff2_in_2, w_ff2_out_2, g_ple_2, w_ple_gate_2, w_ple_proj_2, g_final_2,
):
    x = first_block(
        x, c, ctx, c_ctx, w_mod, b_mod, norm_gain, w_in, conv_w, a_log, dt_bias, dn_norm_gain,
        pool_w, pool_scale, w_out, final_gain,
    )
    return second_block(
        x, p_2, g_ff1_2, w_ff1_in_2, w_ff1_out_2, g_mix_2, w_in_2, b_f_2, w_attn_out_2,
        conv_w_2, conv_b_2, g_conv_2, w_conv_out_2, w_out_2, g_ff2_2, w_ff2_in_2, w_ff2_out_2,
        g_ple_2, w_ple_gate_2, w_ple_proj_2, g_final_2,
    )


_drawn_inputs = setup_inputs


def setup_inputs(seed=0):
    import zlib

    import numpy as np

    out = dict(_drawn_inputs(seed))
    spreads = {}
    factors = {'ctx': 3.077, 'c_ctx': 3.66, 'b_mod': 4.848, 'conv_b_2': 3.861, 'g_ple_2': 5.145}
    for name, (base, spread) in spreads.items():
        noise = np.random.default_rng([zlib.crc32(name.encode()), seed]).standard_normal(out[name].shape)
        drawn = base * np.exp(spread * noise) if base else spread * noise
        out[name] = __import__('jax').numpy.asarray(drawn.astype(out[name].dtype))
    for name, factor in factors.items():
        out[name] = (out[name] * factor).astype(out[name].dtype)
    return out
```

```python
from collections import namedtuple
from contextlib import ExitStack

import numpy as np

import concourse.bass as bass
from concourse import mybir

F32 = mybir.dt.float32
F32R = mybir.dt.float32r
ACT = mybir.ActivationFunctionType
ALU = mybir.AluOpType
AX = mybir.AxisListType


class Names:
    pass


def hold(engine, S):
    engine.sem_inc(S.held, 1)


class Chain:

    def __init__(self, engine, sem):
        self.engine, self.sem, self.base, self.n = engine, sem, 0, 0

    def link(self, ins):
        ins.then_inc(self.sem, 1)
        self.n += 1
        self.engine.wait_ge(self.sem, self.base + self.n)

    def enter(self, i, per):
        assert self.n == 0
        self.base = per * i

    def leave(self, turns, per):
        assert self.n == per, (self.n, per)
        self.n = 0

D = 1024
EPS = 1e-6
LAYERS = 2
D_FF = 2816
FT = D_FF // 128
FFN_RES = 0.5
HEAD_DIM_2 = 64
CONV_TAPS = 31
FCHAIN = 7
CREDIT = 2
NEG_CREDIT = 8
LAYER_SLABS = (("ff1in", 2 * FT, 2 * FT), ("ff1out", 16, 8), ("c", 8, 8), ("at", 24, 24), ("gr", 4, 4), ("am", 8, 8),
               ("wo", 8, 8), ("ff2in", 2 * FT, 2 * FT), ("ff2out", 16, 8), ("ple", 8, 8))


def layer_place(phase, column):
    n = 0
    for row in LAYER_SLABS:
        if row[0] == phase:
            return n
        n += row[column]
    return n


def make_common(nc, K, first_slab, first_evic, split_from):
    S = K.S
    K.layer_slab, K.layer_evic = first_slab, first_evic
    slabs, evics = layer_place(None, 1), layer_place(None, 2)
    K.slab = lambda l, phase: first_slab + slabs * l + layer_place(phase, 1)
    K.evic = lambda l, phase: first_evic + evics * l + layer_place(phase, 2)

    def stream(sp, s0, source, n, l, cols, start=0):
        with sp.Fori(0, n // 2) as i:
            for slot in range(2):
                s = s0 + 2 * i + slot
                sp.wait_ge(S.raw_read, s - 1 + CREDIT)
                sp.dma_start(K.raw[:, slot, 0:cols], source[n * l + start + 2 * i + slot, :, :])\
                    .then_inc(S.raw_full[slot], 16)
    K.stream = stream

    def split_hi(act, s, slot, cols):
        act.wait_ge(S.raw_full[slot], 8 * (s - slot) + 16)
        act.wait_ge(S.slab_done, s + 1)
        nc.scalar.activation(K.wh[:, slot, 0:cols], K.raw[:, slot, 0:cols], ACT.Copy).then_inc(S.wh_ready, 1)

    def split_lo(dve, s, slot, cols):
        dve.wait_ge(S.wh_ready, s + 1 - split_from)
        nc.vector.tensor_tensor(K.wl[:, slot, 0:cols], K.raw[:, slot, 0:cols], K.wh[:, slot, 0:cols].bitcast(F32),
                                ALU.subtract).then_inc(S.raw_read, 1)
    K.split_hi, K.split_lo = split_hi, split_lo

    def mm3(out, slot, unit, xh, xl, start, stop):
        a, b = 128 * unit, 128 * unit + 128
        nc.tensor.matmul(out, K.wh[:, slot, a:b], xh, start=start, stop=False)
        nc.tensor.matmul(out, K.wh[:, slot, a:b], xl, start=False, stop=False)
        return nc.tensor.matmul(out, K.wl[:, slot, a:b], xh, start=False, stop=stop)
    K.mm3 = mm3


def make_layer_memory(nc, K, at):
    def put(name, shape, dtype=F32, where=None):
        nonlocal at
        size = 4 * int(np.prod(shape[1:]))
        offset = at if where is None else where
        t = nc.alloc_sbuf_tensor_at(name, shape, dtype, offset=offset)
        if where is None:
            at += -(-size // 32) * 32
        return t
    K.gains = put("gains", [128, 8 * (4 * LAYERS + 1)])
    K.cw = put("conv_taps", [128, LAYERS * 4 * CONV_TAPS])
    K.cbias = put("conv_bias", [128, LAYERS * 4])
    K.gconv = put("conv_gain", [128, LAYERS * 4])
    K.bf = put("forget_bias", [8, LAYERS])
    K.future = put("future", [128, 128])
    K.wf = put("forget_weights", [128, 8, 8])
    K.negmax = put("negmax", [128, 8])
    K.rowsum = put("rowsum", [128, 8])
    K.rowinv = put("rowinv", [128, 8])
    K.layer_x = at
    K.xgh = put("x_hi", [128, 8, 512], F32R)
    K.xgl = put("x_lo", [128, 8, 512], F32R)
    K.rstd = put("rstd", [128, 512])
    K.std = K.pb[7]
    K.sqsum = put("square_sum", [128, 512])
    K.sqtmp = put("squares", [128, 512])
    u = at
    K.layer_u = u
    K.hid_h = put("hidden_hi", [128, FT, 512], F32R)
    K.hid_l = put("hidden_lo", [128, FT, 512], F32R)
    K.gates = put("gates", [128, 16, 512], F32, u)
    K.mg_h = put("merged_hi", [128, 8, 512], F32R, u)
    K.mg_l = put("merged_lo", [128, 8, 512], F32R, u + 16384)
    K.glu = put("glu", [128, 4, 30 + 512], F32, u + 32768)
    K.cy = put("conv_out", [128, 4, 512], F32, u + 32768 + 8672)
    K.ao_h = put("attended_hi", [128, 4, 512], F32R, u + 49632)
    K.ao_l = put("attended_lo", [128, 4, 512], F32R, u + 57824)
    K.cv_h = put("conved_hi", [128, 4, 512], F32R, u + 66016)
    K.cv_l = put("conved_lo", [128, 4, 512], F32R, u + 74208)
    K.outt = put("out_tiles", [128, 8, 512], F32, u)
    K.crstd = put("conv_rstd", [128, 512], F32, u + 82400)
    K.cm = put("head_forget", [8, 512], F32, u + 84448)
    K.fc = put("forget_sum", [8, 512], F32, u + 86496)
    assert 86496 + 2048 <= 2 * 45056
    x = at
    K.qt = put("queries", [128, 512])
    K.kt = put("keys", [128, 512])
    K.vt = put("values", [128, 512])
    K.vtok = put("values_by_token", [128, 4, 128])
    K.wf_h = put("forget_hi", [128, 8, 128], F32R, x)
    K.wf_l = put("forget_lo", [128, 8, 128], F32R, x + 4096)
    K.p_h = put("embed_hi", [128, 2, 512], F32R, x)
    K.p_l = put("embed_lo", [128, 2, 512], F32R, x + 4096)
    y = at
    K.cb = [put("forget_rows0", [128, 512]), put("forget_rows1", [128, 512])]
    K.p_in = put("embed_in", [128, 2, 512], F32, y)
    z = at
    K.lg = [put("logits0", [128, 512]), put("logits1", [128, 512])]
    K.pr = [put("probs0", [128, 512]), put("probs1", [128, 512])]
    K.fx = put("forget_logits", [8, 512], F32, z)
    K.fe = put("forget_exp", [8, 512], F32, z + 2048)
    K.onerow = put("ones_row", [8, 512], F32, z + 4096)
    w = at
    K.pt = put("probs_by_key", [128, 4, 512])
    K.t1 = put("t1", [128, 512], F32, w)
    K.t2 = put("t2", [128, 512], F32, w + 2048)
    K.silu = put("silu", [128, 512], F32, w + 4096)
    K.g = put("g", [128, 512], F32, w + 6144)
    K.sig = [(K.t1, K.t2), (K.pr[0], K.pr[1])]
    K.ma = put("merge_attention", [128, 512], F32, z)
    K.mc = put("merge_convolution", [128, 512], F32, z + 2048)
    return at

SEMS = ("held started slab_done evac raw_read wh_ready xgh_ready xg_ready ss_ready std_ready rstd_ready "
        "sq_zeroed sq_made sq_added silu_ready g_ready hidh_ready hid_ready forget_step tap_done "
        "wf_zero wf_raw wfh_ready wf_ready edge_zero fl_ready fa_ready fe_ready fln_ready glus_ready glu_ready "
        "cm_ready cbp_ready cb_ready vt_ready vtok_ready sc_ready neg_ready pe_ready ri_ready pn_ready ptp_ready "
        "ptc_ready at_ready aoh_ready ao_ready sq_zeroed2 sq_made2 sq_added2 css_ready cstd_ready crstd_ready cn_ready "
        "cs_ready cvh_ready cv_ready sa_ready ma_ready merged mgh_ready mg_ready p_raw ph_ready pl_ready "
        "gt_ready gs_ready gu_ready out_ready out_done "
        "cond_in x_in cond_ready wabh_ready wab_ready ssq_ready ssum sss_ready sstd_ready srstd_ready mod_ready sxn_ready "
        "shn_ready hnh_ready hn_ready ab_ready alog_ready gabs_ready gexp_ready gln_ready lg_ready "
        "cums_ready step_gates gate_step short_step center_ready head_ready tk_ready hsq_ready hstd_ready hr_ready tv_ready "
        "vs_ready kqn_ready kb_ready kq_ready ks_ready gb_ready dg_ready eg_ready arg_ready dec_ready decm_ready "
        "kk_ready qkd_ready bd_ready bt_ready e0_ready es_ready e_ready tt_ready dd_ready bl_ready p_ready pp_ready w_ready "
        "qd_ready sk_ready rr_ready sx_ready vn_ready se_ready su_ready sd_used st_ready so_ready ot_ready osq_ready "
        "oss_ready ostd_ready orstd_ready on_ready pooled pad_step box_step icnt_in dh_ready d_ready zs_used "
        "yh_ready y_ready res_ready fsq_step fss_ready fstd_ready frstd_ready").split()

Semaphores = namedtuple("Semaphores", SEMS + ["raw_full"])


def make_sems(nc, ctx):
    raw_full = [ctx.enter_context(nc.semaphore("raw_full0")), ctx.enter_context(nc.semaphore("raw_full1"))]
    return Semaphores(*[ctx.enter_context(nc.semaphore(n)) for n in SEMS], raw_full)


def start_credits(pool, S):
    for s in (S.slab_done, S.evac, S.raw_read, S.std_ready, S.rstd_ready, S.sq_added, S.silu_ready, S.g_ready,
              S.hid_ready, S.wf_ready, S.glu_ready, S.cbp_ready, S.vtok_ready, S.pe_ready, S.ptp_ready, S.ptc_ready,
              S.at_ready, S.ao_ready, S.merged, S.gu_ready,
              S.head_ready, S.kqn_ready, S.kb_ready, S.kq_ready, S.bt_ready, S.qd_ready, S.dd_ready, S.bl_ready,
              S.p_ready, S.pp_ready, S.w_ready, S.ks_ready, S.vs_ready, S.e_ready):
        pool.sem_inc(s, CREDIT)
    pool.sem_inc(S.slab_done, FIRST_RAW)
    pool.sem_inc(S.neg_ready, NEG_CREDIT)
    pool.sem_inc(S.started, 1)


def make_shared_memory(nc, K, ctx):
    at = -(-nc.sbuf_base // 32) * 32

    def put(name, shape, dtype=F32):
        nonlocal at
        t = nc.alloc_sbuf_tensor_at(name, shape, dtype, offset=at)
        at += -(-4 * int(np.prod(shape[1:])) // 32) * 32
        return t
    K.h = put("h", [128, 8, 512])
    K.wbase = at
    K.raw = put("weights_raw", [128, 2, 1408])
    K.wh = put("weights_hi", [128, 2, 1408], F32R)
    K.wl = put("weights_lo", [128, 2, 1408], F32R)
    K.ident = put("identity", [128, 128])
    K.ones = put("ones", [128, 128])
    K.eps = put("eps", [128, 1])
    K.pb = [ctx.enter_context(nc.psum_tensor(f"bank{i}", [128, 512], F32)) for i in range(8)]
    return at


def tape(w, order=None, k=None):
    kt = w.shape[0] // 128
    t = w.reshape(kt, 128, -1, 128).transpose(2, 1, 0, 3)
    if order is not None:
        t = t[order]
    return t.reshape(t.shape[0], 128, kt * 128)


def long_tape(w, parts):
    kt = w.shape[0] // 128
    t = w.reshape(parts, kt // parts, 128, -1, 128).transpose(3, 0, 2, 1, 4)
    return t.reshape(t.shape[0] * parts, 128, -1)


def columns(v):
    return np.ascontiguousarray(v.reshape(-1, 128).T)


def layer_arrays(A):
    r = {}
    L = LAYERS
    half = [x for i in range(FT) for x in (i, FT + i)]
    mixer = [x for i in range(4) for x in (12 + i, 16 + i)]
    for p in range(4):
        mixer += [p, 4 + p, 8 + p, 20 + 3 * p, 21 + 3 * p, 22 + 3 * p]
    mixer += [32, 33, 34, 35]
    w_in = A["w_in_2"]
    f0 = 3 * 512
    no_f = np.concatenate([w_in[:, :, :f0], w_in[:, :, f0 + 8:]], axis=2)
    r["w_f"] = w_in[:, :, f0:f0 + 8].reshape(L, 8, 128, 8).transpose(0, 2, 1, 3).reshape(L, 128, 64)
    r["w_mix"] = np.concatenate([tape(no_f[l], mixer) for l in range(L)])
    for n in ("ff1", "ff2"):
        r[f"w_{n}in"] = np.concatenate([tape(A[f"w_{n}_in_2"][l], half) for l in range(L)])
        r[f"w_{n}out"] = np.concatenate([long_tape(A[f"w_{n}_out_2"][l], 2) for l in range(L)])
    r["w_am"] = np.concatenate([tape(np.concatenate([A["w_attn_out_2"][l], A["w_conv_out_2"][l]])) for l in range(L)])
    r["w_wo"] = np.concatenate([tape(A["w_out_2"][l]) for l in range(L)])
    r["w_ple"] = np.concatenate([tape(np.concatenate([A["w_ple_gate_2"][l], A["w_ple_proj_2"][l]])) for l in range(L)])
    r["p_t"] = A["p_2"][:, 0].transpose(0, 2, 1).reshape(L, 2, 128, 512).transpose(0, 2, 1, 3).reshape(L, 128, 1024)
    gains = []
    for l in range(L):
        gains += [A["g_ff1_2"][l], A["g_mix_2"][l], A["g_ff2_2"][l], A["g_ple_2"][l]]
    gains.append(A["g_final_2"])
    r["gains"] = columns(np.stack(gains))
    r["cw"] = A["conv_w_2"].reshape(L, CONV_TAPS, 4, 128).transpose(3, 0, 2, 1).reshape(128, -1)
    r["cbias"] = columns(A["conv_b_2"])
    r["gconv"] = columns(A["g_conv_2"])
    r["bf"] = A["b_f_2"].T
    return {k: np.ascontiguousarray(v) for k, v in r.items()}


def const_arrays():
    i = np.arange(128)
    return {
        "c_ident": np.eye(128, dtype=np.float32),
        "c_ones": np.ones((128, 128), np.float32),
        "c_future": np.where(i[None, :] > i[:, None], np.float32(1e30), np.float32(0)),
        "c_eps": np.full((128, 1), EPS, np.float32),
    }

HEADS = 8
GROUPS = 4
TOK = 512
CTX = 256
ALLT = TOK + CTX
TILES = ALLT // 128
CHUNK = 128
LEVELS = 7
SHORT = 5
HEAD_SLABS = ((0, 0), (1, 0), (2, 0), (1, 1), (2, 1), (0, 1))
MOD_SLABS = 24
DN_SLAB = MOD_SLABS
TAIL_SLAB = DN_SLAB + 24
TAIL_SLABS = 26
OUT_SLAB = TAIL_SLAB + TAIL_SLABS
LAYER_SLAB = OUT_SLAB + 16
DN_EVIC, TAIL_EVIC, OUT_EVIC, LAYER_EVIC = 0, 24, 50, 58
WINDOWS = (2, 4, 8, 16)
GRID_W, GRID_H = 64, 8
PADW = GRID_W + 16
CONV_STEPS = 2 * (3 + 7 + 7)
FIRST_RAW = MOD_SLABS
TAIL = (("u", 0), ("z", 0), ("u", 1), ("z", 1), ("u", 2), ("z", 2), ("u", 3), ("z", 3), ("u", 4), ("z", 4), ("w", 0),
        ("p", 0), ("u", 5), ("z", 5), ("p", 1), ("u", 6), ("z", 6), ("p", 2), ("u", 7), ("z", 7), ("p", 3), ("w", 1),
        ("p", 4), ("p", 5), ("p", 6), ("p", 7))
OUT_ORDER = tuple(m + 8 * (kind == "p") for kind, m in TAIL if kind in "zp")
SPLIT_AT = {min(TAIL.index(("u", m)) + 3, TAIL.index(("w", m // 4)) - 1 if m % 4 == 3 else 99): m for m in range(8)}
SBUF_END = 229376


def wide(ap, axis, n):
    a = ap.unsqueeze(axis)
    shape = list(a.shape)
    shape[axis] = n
    return a.to_broadcast(shape)


def make_first_memory(nc, K, at):
    def put(name, shape, dtype=F32, where=None):
        nonlocal at
        size = -(-4 * int(np.prod(shape[1:])) // 32) * 32
        t = nc.alloc_sbuf_tensor_at(name, shape, dtype, offset=at if where is None else where)
        if where is None:
            at += size
        return t
    gaps = [K.wbase + t * 11264 + s * 5632 + 4096 for t in range(3) for s in range(2)]
    K.level = [put(f"level_mask{l}", [128, 2, 128], F32, gaps[l]) for l in range(LEVELS - 1)]
    K.incl = [put(f"chunk_mask{d}", [128, 128], F32, gaps[d] + 1024) for d in range(2)]
    K.wk = put("short_taps", [128, 24 * SHORT], F32, gaps[2] + 1024)
    K.negeg = put("minus_exp_sum", [128, TILES, 16], F32, gaps[3] + 1024)
    K.tail_s = put("tail_decay", [128, TILES, 16], F32, gaps[4] + 1024)
    hn = K.layer_x
    K.hnh = put("normed_hi", [128, 8, ALLT], F32R, hn)
    K.hnl = put("normed_lo", [128, 8, ALLT], F32R, hn + 24576)
    at = hn + 49152
    ot = at
    K.ot = put("delta_out", [128, HEADS, TOK])
    masks = at
    K.level.append(put(f"level_mask{LEVELS - 1}", [128, 2, 128]))
    K.cum = put("log_decay_sum", [128, TILES, 16])
    K.logd = put("log_decay", [128, TILES, 16])
    K.beta = put("beta", [128, TILES, 16])
    K.etot = put("chunk_decay", [128, TILES, 16])
    K.fgain = put("block_gain", [128, 8])
    K.cvec = put("condition", [128, 8, 2])
    K.bmod = put("mod_bias", [128, 24])
    K.modv = put("modulation", [128, 24, 2])
    K.ngain = put("norm_gain", [128, 8])
    K.dngain = put("delta_gain", [128, 1])
    K.pscale = put("pool_scale", [128, 8])
    K.epsq = put("eps_scaled", [128, 1])
    K.ssq = put("head_squares", [128, TILES, 4])
    g0 = at
    K.kq = put("keys_queries", [128, TILES, 4, 128])
    K.vs = put("values", [128, TILES, 2, 128])
    K.ks = put("decayed_keys", [128, TILES, 4, 128])
    K.e = put("inverse", [128, TILES, 4, 128])
    K.qkd = put("decayed_scores", [128, 4, 4, 128])
    K.qd = put("decayed_queries", [128, 4, 4, 128])
    w0 = at
    bt_late = at
    at += 6144
    K.dd = put("inverse_turned", [128, 3, 4, 128])
    K.pp = put("product", [128, 2, 4, 128])
    K.bl = put("level_part", [128, 2, 4, 128])
    K.dec = put("decay", [128, 4, 128])
    K.dg = put("diagonal", [128, 4, 128])
    K.bt = [put(f"system{t}", [128, 4, 128], F32, at + 2048 * t) for t in range(3)]
    K.bt += [put(f"system{t}", [128, 4, 128], F32, bt_late + 2048 * (t - 3)) for t in range(3, TILES)]
    K.st = put("state", [128, 4, 128])
    K.rr = put("residual", [128, 4, 128])
    K.vn = put("new_values", [128, 4, 128])
    end = at
    K.hv = [put(f"head{j}_{'qkv'[kind]}", [128, ALLT], F32, w0 + i * 3072) for i, (kind, j) in enumerate(HEAD_SLABS)]
    K.acc = [put(f"short_conv{i}", [128, ALLT], F32, w0 + 18432 + 3072 * i) for i in range(2)]
    K.kqn = [put(f"unit_keys{i}", [128, 4, 128], F32, w0 + 18432 + 2048 * i) for i in range(2)]
    K.junk = put("square_junk", [128, 128], F32, w0 + 22528)
    K.ctx = put("context", [128, 8, CTX], F32, g0)
    K.sacc = put("start_square_sum", [128, ALLT], F32, g0 + 8192)
    K.ssqt = [put(f"start_squares{i}", [128, ALLT], F32, g0 + 11264 + 3072 * i) for i in range(2)]
    K.srstd = put("start_rstd", [128, ALLT], F32, g0 + 17408)
    K.shn = [put(f"start_normed{i}", [128, ALLT], F32, g0 + 20480 + 3072 * i) for i in range(2)]
    K.sxn = [put(f"start_scaled{i}", [128, ALLT], F32, g0 + 26624 + 3072 * i) for i in range(2)]
    K.wab = put("gate_weights", [128, 8, 32], F32, g0 + 32768)
    K.wabh = put("gate_weights_hi", [128, 8, 32], F32R, g0 + 33792)
    K.wabl = put("gate_weights_lo", [128, 8, 32], F32R, g0 + 34816)
    K.alog = put("a_log", [128, 16], F32, g0 + 35840)
    K.dtb = put("dt_bias", [128, 16], F32, g0 + 35904)
    K.gsum = put("gate_a", [128, TILES, 16], F32, g0 + 36864)
    K.gexp = put("gate_b", [128, TILES, 16], F32, g0 + 37248)
    K.gneg = put("gate_c", [128, TILES, 16], F32, g0 + 37632)
    K.modp = put("mod_scale", [128, 8, 2], F32, g0 + 38016)
    K.yh = [put(f"mixed_hi{m}", [128, TOK], F32R, ot + 2048 * m if m < 8 else g0 + 2048 * (m - 8)) for m in range(16)]
    K.yl = [put(f"mixed_lo{m}", [128, TOK], F32R, g0 + 16384 + 2048 * m) for m in range(16)]
    t0 = g0 + 49152
    K.dh = put("pooled_hi", [128, 4, TOK], F32R, t0)
    K.dl = put("pooled_lo", [128, 4, TOK], F32R, t0 + 8192)
    K.ypre = put("pool_mixed", [128, 4, TOK], F32, t0 + 16384)
    K.upad = [put(f"grid{i}", [128, GRID_H, PADW], F32, t0 + 24576 + 2560 * i) for i in range(3)]
    K.box = put("box", [128, GRID_H, GRID_W], F32, t0 + 32256)
    K.icnt = put("count_inverse", [128, TOK], F32, t0 + 34304)
    K.ytmp = put("head_gated", [128, TOK], F32, t0 + 36352)
    K.zs = put("gate_silu", [128, TOK], F32, masks)
    K.os = put("head_square", [128, TOK], F32, t0 + 38400)
    assert t0 + 40448 <= end
    assert end <= SBUF_END, end


def scan_steps():
    yield 4, 5, None
    yield 5, 4, None
    for i in range(4):
        yield i, 3 - i, i


def delta_block(K):
    nc, S = K.nc, K.S
    pb, h = K.pb, K.h
    split_hi, split_lo, mm3 = K.split_hi, K.split_lo, K.mm3
    hnh, hnl = K.hnh, K.hnl

    def sp_prog(sp):
        sp.dma_start(K.cvec[:, :, :], K.cond).then_inc(S.cond_in, 16)
        K.stream(sp, 0, K.w_mod, MOD_SLABS, 0, 1024)
        K.stream(sp, DN_SLAB, K.w_dn, 24, 0, 1024)
        K.stream(sp, TAIL_SLAB, K.w_tail, TAIL_SLABS, 0, 1024)
        K.stream(sp, OUT_SLAB, K.w_out1, 16, 0, 1024)

    def act_start(act):
        for dst, src in K.consts_act:
            act.dma_start(dst, src).then_inc(S.x_in, 16)
        act.wait_ge(S.cond_in, 16)
        nc.scalar.activation(K.cvec[:, :, :], K.cvec[:, :, :], ACT.Silu).then_inc(S.cond_ready, 1)
        act.wait_ge(S.x_in, 16 * len(K.consts_act))
        nc.scalar.activation(K.wabh[:, :, :], K.wab[:, :, :], ACT.Copy).then_inc(S.wabh_ready, 1)
        for m in range(8):
            if m >= 2:
                act.wait_ge(S.ssum, 2 * (m - 1))
            nc.scalar.activation(K.ssqt[m % 2][:, 0:TOK], h[:, m, :], ACT.Square).then_inc(S.ssq_ready, 1)
            nc.scalar.activation(K.ssqt[m % 2][:, TOK:ALLT], K.ctx[:, m, :], ACT.Square).then_inc(S.ssq_ready, 1)
        for n, w in ((0, TOK), (1, CTX)):
            act.wait_ge(S.sss_ready, n + 1)
            nc.scalar.activation(pb[4 + n][:, 0:w], pb[4 + n][:, 0:w], ACT.Sqrt, bias=K.eps[:, 0:1], scale=1.0 / D)\
                .then_inc(S.sstd_ready, 1)
        act.wait_ge(S.mod_ready, 3)
        for m in range(8):
            for n, (a, b) in enumerate(((0, TOK), (TOK, ALLT))):
                act.wait_ge(S.sxn_ready, 2 * m + n + 1)
                if m >= 2:
                    act.wait_ge(S.hn_ready, 2 * (m - 2) + n + 1)
                nc.scalar.activation(K.shn[m % 2][:, a:b], K.sxn[m % 2][:, a:b], ACT.Identity,
                                     scale=K.modp[:, m, n:n + 1], bias=K.modv[:, m, n:n + 1]).then_inc(S.shn_ready, 1)
            for n, (a, b) in enumerate(((0, TOK), (TOK, ALLT))):
                act.wait_ge(S.shn_ready, 2 * m + n + 1)
                nc.scalar.activation(hnh[:, m, a:b], K.shn[m % 2][:, a:b], ACT.Copy).then_inc(S.hnh_ready, 1)
        split_hi(act, DN_SLAB, 0, 1024)
        split_hi(act, DN_SLAB + 1, 1, 1024)

    def act_gates(act):
        act.wait_ge(S.gate_step, 1)
        nc.scalar.activation(K.beta[:, :, :], pb[6][:, 0:192].rearrange("p (t c) -> p t c", c=32)[:, :, 16:32],
                             ACT.Sigmoid)
        nc.scalar.activation(K.alog[:, :], K.alog[:, :], ACT.Exp).then_inc(S.alog_ready, 1)
        act.wait_ge(S.gabs_ready, 1)
        nc.scalar.activation(K.gexp[:, :, :], K.gexp[:, :, :], ACT.Exp, scale=-1.0).then_inc(S.gexp_ready, 1)
        act.wait_ge(S.gexp_ready, 1)
        nc.scalar.activation(K.gexp[:, :, :], K.gexp[:, :, :], ACT.Ln, bias=1.0).then_inc(S.gln_ready, 1)

    def act_sums(act):
        act.wait_ge(S.gate_step, 6)
        nc.scalar.activation(K.etot[:, :, :], pb[7][:, 96:192].rearrange("p (t c) -> p t c", c=16), ACT.Exp)\
            .then_inc(S.step_gates, 1)
        nc.scalar.activation(K.negeg[:, :, :], K.cum[:, :, :], ACT.Exp).then_inc(S.step_gates, 1)
        nc.scalar.activation(K.tail_s[:, :, :], K.tail_s[:, :, :], ACT.Exp).then_inc(S.step_gates, 1)

    def act_project(act, G, first=False):
        s = DN_SLAB + 6 * G
        for i in range(6):
            kind = HEAD_SLABS[i][0]
            split_hi(act, s + i + 2, i % 2, 1024)
            act.wait_ge(S.slab_done, s + i + 1 + CREDIT)
            act.wait_ge(S.head_ready, 6 * G + i - 1 + CREDIT)
            hold(act, S)
            col = K.wk[:, bass.ds(10 * G + SHORT * (8 * kind + HEAD_SLABS[i][1]) + 2, 1)]
            for lo, bank in ((0, pb[i % 2]),) if kind == 0 else ((0, pb[i % 2]), (TOK, pb[2 + i % 2])):
                hi = ALLT if lo else TOK
                ins = nc.scalar.activation(K.acc[i % 2][:, lo:hi], bank[:, 0:hi - lo], ACT.Copy, scale=col)
            ins.then_inc(S.center_ready, 1)
            act.wait_ge(S.evac, DN_EVIC + 6 * G + i + 1 + CREDIT)
            w = TOK if kind == 0 else ALLT
            nc.scalar.activation(K.hv[i][:, 0:w], K.acc[i % 2][:, 0:w], ACT.Silu).then_inc(S.head_ready, 1)
            if first and i == 1:
                act_gates(act)
            if first and i == 3:
                act_sums(act)

    def act_solve(act, G):
        def squares(t):
            n = TILES * G + t
            w = 4 if t < 4 else 2
            act.wait_ge(S.tk_ready, n + 1)
            for c in range(w):
                nc.scalar.activation(K.junk[:, :], pb[t % 2][:, 128 * c:128 * c + 128], ACT.Square,
                                     accum_out=K.ssq[:, t, c:c + 1]).then_inc(S.hsq_ready, 1)
                act.wait_ge(S.hsq_ready, 20 * G + 4 * min(t, 4) + 2 * max(t - 4, 0) + c + 1)
            nc.scalar.activation(K.ssq[:, t, 0:2], K.ssq[:, t, 0:2], ACT.Sqrt, bias=K.eps[:, 0:1]).then_inc(S.hstd_ready, 1)
            if t < 4:
                nc.scalar.activation(K.ssq[:, t, 2:4], K.ssq[:, t, 2:4], ACT.Sqrt, bias=K.epsq[:, 0:1], scale=128.0)\
                    .then_inc(S.hstd_ready, 1)
            act.wait_ge(S.tv_ready, n + 1)
            nc.scalar.activation(K.vs[:, t, :, :], pb[2 + t % 2][:, 0:256].rearrange("p (j v) -> p j v", v=128), ACT.Copy)\
                .then_inc(S.vs_ready, 1)

        def keys_back(t):
            n = TILES * G + t
            w = 4 if t < 4 else 2
            act.wait_ge(S.kb_ready, n + 1 + CREDIT)
            nc.scalar.activation(K.kq[:, t, 0:w, :], pb[4 + t % 2][:, 0:128 * w].rearrange("p (c v) -> p c v", v=128),
                                 ACT.Copy).then_inc(S.kq_ready, 1)
        squares(0)
        for t in range(1, TILES):
            squares(t)
            keys_back(t - 1)
        keys_back(TILES - 1)

        def setup(t):
            n = TILES * G + t
            act.wait_ge(S.arg_ready, 4 * n + 4)
            nc.scalar.activation(dec_of(t), dec_of(t), ACT.Exp).then_inc(S.dec_ready, 1)
            if t < 4:
                nc.scalar.activation(dg_of(t), sum_bank(t)[:, :].rearrange("p (c v) -> p c v", v=128), ACT.Exp)\
                    .then_inc(S.eg_ready, 1)

        def turned(hb, l, i):
            act.wait_ge(S.tt_ready, 36 * G + 18 * hb + 3 * l + i + 1)
            nc.scalar.activation(K.dd[:, i, :, :], pb[6 + turn_par(l, i)][:, :].rearrange("p (c v) -> p c v", v=128),
                                 ACT.Copy).then_inc(S.dd_ready, 1)
        for i in range(3):
            setup(i)
        for i in range(3):
            turned(0, 0, i)
        for hb in range(2):
            if hb == 1:
                for i in range(3):
                    turned(1, 0, i)
            for l in range(1, LEVELS):
                for i in range(3):
                    c = 36 * G + 18 * hb + 3 * (l - 1) + i
                    act.wait_ge(S.p_ready, c + 1 + CREDIT)
                    act.wait_ge(S.w_ready, c - 1 + CREDIT)
                    nc.scalar.activation(K.pp[:, c_par(l, i), :, :], pb[c_par(l, i)][:, :].rearrange("p (c v) -> p c v", v=128),
                                         ACT.Copy).then_inc(S.pp_ready, 1)
                if l < LEVELS - 1:
                    for i in range(3):
                        turned(hb, l, i)
                if hb == 0 and l % 2 == 1:
                    setup(3 + l // 2)

    def dg_of(t):
        return K.pp[:, t - 1, :, :] if t in (1, 2) else K.dg[:, :, :]

    def dec_of(t):
        return K.bl[:, t - 1, :, :] if t in (1, 2) else K.dec[:, :, :]

    def sum_bank(t):
        return pb[(4, 0, 2)[t] if t < 3 else 4]

    def key_bank(t):
        return pb[(5, 1, 3)[t] if t < 3 else 5]

    def c_par(l, i):
        return (3 * (l - 1) + i) % 2

    def turn_par(l, i):
        return (3 * l + i) % 2

    def act_tail(act):
        act.wait_ge(S.ot_ready, 8 * GROUPS)
        n = 0
        for i, (kind, m) in enumerate(TAIL):
            a = TAIL_SLAB + i
            slot = a % 2
            if kind == "u":
                if m > 0:
                    act.wait_ge(S.oss_ready, m)
                nc.scalar.activation(K.os[:, :], K.ot[:, m, :], ACT.Square).then_inc(S.osq_ready, 1)
            split_hi(act, a + 2, slot, 1024)
            act.wait_ge(S.slab_done, a + 1 + CREDIT)
            if kind == "u":
                act.wait_ge(S.pad_step, 3)
                if m > 0:
                    act.wait_ge(S.pooled, m)
                nc.scalar.activation(K.upad[0][:, :, 8:8 + GRID_W], pb[slot][:, :].rearrange("p (r c) -> p r c", c=GRID_W),
                                     ACT.Copy).then_inc(S.evac, 1)
                act.wait_ge(S.oss_ready, m + 1)
                nc.scalar.activation(pb[5][:, :], pb[5][:, :], ACT.Sqrt, bias=K.eps[:, 0:1], scale=1.0 / 128)\
                    .then_inc(S.ostd_ready, 1)
            elif kind == "w":
                if m > 0:
                    act.wait_ge(S.y_ready, 12)
                for q in range(4):
                    ins = nc.scalar.activation(K.ypre[:, q, :], pb[(2, 3, 6, 7)[q]][:, :], ACT.Copy,
                                               scale=K.pscale[:, 4 * m + q:4 * m + q + 1])
                ins.then_inc(S.evac, 1)
            else:
                if n > 0:
                    act.wait_ge(S.zs_used, n)
                nc.scalar.activation(K.zs[:, :], pb[slot][:, :], ACT.Silu).then_inc(S.evac, 1)
                n += 1
                act.wait_ge(S.zs_used, n)
                if kind == "z":
                    nc.scalar.activation(K.yh[m][:, :], K.ytmp[:, :], ACT.Copy).then_inc(S.yh_ready, 1)
                else:
                    nc.scalar.activation(K.yh[8 + m][:, :], K.ypre[:, m % 4, :], ACT.Copy).then_inc(S.yh_ready, 1)
            if i in SPLIT_AT:
                m = SPLIT_AT[i]
                act.wait_ge(S.pooled, m + 1)
                nc.scalar.activation(K.dh[:, m % 4, :], K.box[:, :, :].rearrange("p r c -> p (r c)"), ACT.Copy)\
                    .then_inc(S.dh_ready, 1)
        for m in range(8):
            split_hi(act, OUT_SLAB + 2 * m + 2, 0, 1024)
            split_hi(act, OUT_SLAB + 2 * m + 3, 1, 1024)
        act.wait_ge(S.fss_ready, 1)
        nc.scalar.activation(K.std[:, :], pb[7][:, :], ACT.Sqrt, bias=K.eps[:, 0:1], scale=1.0 / D).then_inc(S.fstd_ready, 1)
        for m in range(8):
            act.wait_ge(S.evac, OUT_EVIC + m + 1 + CREDIT)
            nc.scalar.activation(K.xgh[:, m, :], h[:, m, :], ACT.Copy, scale=K.gains[:, m:m + 1]).then_inc(S.xgh_ready, 1)

    def act_prog(act):
        act_start(act)
        act_project(act, 0, True)
        with act.Fori(0, GROUPS - 1) as G:
            act_solve(act, G)
            act_project(act, G + 1)
        act_solve(act, GROUPS - 1)
        act_tail(act)

    def dve_start(dve):
        dve.wait_ge(S.started, 1)
        dve.wait_ge(S.wabh_ready, 1)
        nc.vector.tensor_tensor(K.wabl[:, :, :], K.wab[:, :, :], K.wabh[:, :, :].bitcast(F32), ALU.subtract)\
            .then_inc(S.wab_ready, 1)
        for m in range(8):
            for n, (a, b) in enumerate(((0, TOK), (TOK, ALLT))):
                dve.wait_ge(S.ssq_ready, 2 * m + n + 1)
                if m == 0:
                    nc.vector.tensor_copy(K.sacc[:, a:b], K.ssqt[0][:, a:b]).then_inc(S.ssum, 1)
                else:
                    dve.wait_ge(S.ssum, 2 * (m - 1) + n + 1)
                    nc.vector.tensor_tensor(K.sacc[:, a:b], K.sacc[:, a:b], K.ssqt[m % 2][:, a:b], ALU.add)\
                        .then_inc(S.ssum, 1)
        for n, (a, b) in enumerate(((0, TOK), (TOK, ALLT))):
            dve.wait_ge(S.sstd_ready, n + 1)
            nc.vector.reciprocal(K.srstd[:, a:b], pb[4 + n][:, 0:b - a]).then_inc(S.srstd_ready, 1)
        dve.wait_ge(S.raw_read, 16 + CREDIT)
        nc.vector.tensor_tensor(K.modv[:, 0:16, :], pb[7][:, 0:32].rearrange("p (m c) -> p m c", c=2), wide(K.bmod[:, 0:16], 2, 2),
                                ALU.add).then_inc(S.mod_ready, 1)
        dve.wait_ge(S.mod_ready, 1)
        nc.vector.tensor_scalar(K.modp[:, :, :], K.modv[:, 8:16, :], 1.0, None, ALU.add).then_inc(S.mod_ready, 1)
        dve.wait_ge(S.mod_ready, 2)
        nc.vector.tensor_tensor(K.modp[:, :, :], K.modp[:, :, :], wide(K.ngain[:, :], 2, 2), ALU.mult).then_inc(S.mod_ready, 1)
        dve.wait_ge(S.srstd_ready, 2)

        def scaled(m):
            for n, (a, b) in enumerate(((0, TOK), (TOK, ALLT))):
                if m >= 2:
                    dve.wait_ge(S.shn_ready, 2 * (m - 2) + n + 1)
                src = h[:, m, :] if n == 0 else K.ctx[:, m, :]
                nc.vector.tensor_tensor(K.sxn[m % 2][:, a:b], src, K.srstd[:, a:b], ALU.mult).then_inc(S.sxn_ready, 1)

        def low(m):
            for n, (a, b) in enumerate(((0, TOK), (TOK, ALLT))):
                dve.wait_ge(S.hnh_ready, 2 * m + n + 1)
                nc.vector.tensor_tensor(hnl[:, m, a:b], K.shn[m % 2][:, a:b], hnh[:, m, a:b].bitcast(F32), ALU.subtract)\
                    .then_inc(S.hn_ready, 1)
        scaled(0)
        for m in range(1, 8):
            scaled(m)
            low(m - 1)
        low(7)
        dve.wait_ge(S.raw_read, MOD_SLABS + CREDIT)
        nc.vector.tensor_tensor(K.modv[:, 16:24, :], pb[3][:, 0:16].rearrange("p (m c) -> p m c", c=2), wide(K.bmod[:, 16:24], 2, 2),
                                ALU.add).then_inc(S.mod_ready, 1)
        split_lo(dve, DN_SLAB, 0, 1024)
        split_lo(dve, DN_SLAB + 1, 1, 1024)

    def dve_gates(dve):
        ch = K.gatechain
        dve.wait_ge(S.ab_ready, 1)
        a = pb[6][:, 0:192].rearrange("p (t c) -> p t c", c=32)[:, :, 0:16]
        ch.link(nc.vector.tensor_tensor(K.gsum[:, :, :], a, wide(K.dtb[:, :], 1, TILES), ALU.add))
        ch.link(nc.vector.tensor_scalar(K.gneg[:, :, :], K.gsum[:, :, :], -1.0, None, ALU.mult))
        nc.vector.tensor_tensor(K.gexp[:, :, :], K.gsum[:, :, :], K.gneg[:, :, :], ALU.max).then_inc(S.gabs_ready, 1)
        ch.link(nc.vector.tensor_scalar(K.gsum[:, :, :], K.gsum[:, :, :], 0.0, None, ALU.max))
        dve.wait_ge(S.gln_ready, 1)
        ch.link(nc.vector.tensor_tensor(K.gsum[:, :, :], K.gsum[:, :, :], K.gexp[:, :, :], ALU.add))
        dve.wait_ge(S.alog_ready, 1)
        nc.vector.scalar_tensor_tensor(out=K.logd[:, :, :], in0=K.gsum[:, :, :], scalar=-1.0,
                                       in1=wide(K.alog[:, :], 1, TILES), op0=ALU.mult, op1=ALU.mult).then_inc(S.lg_ready, 1)

    def dve_sums(dve):
        ch = K.gatechain
        dve.wait_ge(S.cums_ready, 1)
        ch.link(nc.vector.tensor_copy(K.cum[:, :, :], pb[7][:, 0:96].rearrange("p (t c) -> p t c", c=16)))
        ch.link(nc.vector.tensor_tensor(K.tail_s[:, :, :], pb[7][:, 96:192].rearrange("p (t c) -> p t c", c=16), K.cum[:, :, :],
                                        ALU.subtract))
        dve.wait_ge(S.step_gates, 3)
        ch.link(nc.vector.tensor_scalar(K.negeg[:, :, :], K.negeg[:, :, :], -1.0, None, ALU.mult))

    def heads(t16, G):
        return t16.rearrange("p (d h) -> p d h", h=HEADS)[:, :, bass.ds(2 * G, 2)]

    def conv_ops(dve, G, i):
        conv = K.convchain
        if i == 0:
            conv.enter(G, CONV_STEPS)
        kind, j = HEAD_SLABS[i]
        acc = K.acc[i % 2]
        tile = 8 * kind + j
        dve.wait_ge(S.center_ready, 6 * G + i + 1)
        for base, w, bank in ((0, TOK, pb[i % 2]), (TOK, CTX, pb[2 + i % 2])):
            if base and kind == 0:
                continue
            for k in (0, 1, 3, 4):
                col = K.wk[:, bass.ds(10 * G + SHORT * tile + k, 1)]
                lo, hi = max(0, 2 - k), min(w, w + 2 - k)
                ins = nc.vector.scalar_tensor_tensor(out=acc[:, base + lo:base + hi], in0=bank[:, lo + k - 2:hi + k - 2],
                                                     scalar=col, in1=acc[:, base + lo:base + hi],
                                                     op0=ALU.mult, op1=ALU.add)
                if k == 4 and ((base > 0) or kind == 0):
                    ins.then_inc(S.evac, 1)
                else:
                    conv.link(ins)
                yield
        if i == 5:
            conv.leave(GROUPS, CONV_STEPS)

    def take(ops, n):
        for _ in range(n):
            next(ops, None)

    def dve_solve(dve, G):
        for t in range(TILES):
            n = TILES * G + t
            w = 4 if t < 4 else 2
            dve.wait_ge(S.hstd_ready, 10 * G + (2 * t + 2 if t < 4 else 5 + t))
            nc.vector.reciprocal(K.ssq[:, t, 0:w], K.ssq[:, t, 0:w]).then_inc(S.hr_ready, 1)
            dve.wait_ge(S.hr_ready, n + 1)
            dve.wait_ge(S.kb_ready, n - 1 + CREDIT)
            dve.wait_ge(S.ks_ready, n - 1 + CREDIT)
            nc.vector.tensor_tensor(K.kqn[t % 2][:, 0:w, :], pb[t % 2][:, 0:128 * w].rearrange("p (c v) -> p c v", v=128),
                                    wide(K.ssq[:, t, 0:w], 2, 128), ALU.mult).then_inc(S.kqn_ready, 1)

        def quad(x):
            return x.rearrange("p (d j) c -> p d j c", j=2)

        def setup_a(t):
            dve.wait_ge(S.qd_ready, 4 * G + (min(t, 4) if t > 2 else 0) + CREDIT)
            if t == 0:
                dve.wait_ge(S.vs_ready, TILES * G + TILES + CREDIT)
                dve.wait_ge(S.ks_ready, TILES * G + TILES + CREDIT)
            nc.vector.tensor_tensor(quad(dg_of(t)), wide(wide(K.ident[:, :], 1, 2), 1, 2),
                                    wide(heads(K.cum[:, t, :], G), 3, 128), ALU.mult).then_inc(S.dg_ready, 1)

        def setup_b(t):
            dve.wait_ge(S.gb_ready, TILES * G + t + 1)
            for d in range(2):
                for j in range(2):
                    c = 2 * d + j
                    nc.vector.tensor_scalar(dec_of(t)[:, c, :], sum_bank(t)[:, 128 * c:128 * c + 128],
                                            K.cum[:, t, bass.ds(8 * d + 2 * G + j, 1)], 0.0, ALU.subtract, ALU.min)\
                        .then_inc(S.arg_ready, 1)

        def setup_c(t):
            n = TILES * G + t
            dve.wait_ge(S.dec_ready, n + 1)
            for d in range(2):
                nc.vector.tensor_tensor(dec_of(t)[:, 2 * d:2 * d + 2, :], dec_of(t)[:, 2 * d:2 * d + 2, :],
                                        wide(K.incl[d][:, :], 1, 2), ALU.mult).then_inc(S.decm_ready, 1)
            dve.wait_ge(S.decm_ready, 2 * n + 2)
            if t < 4:
                dve.wait_ge(S.kk_ready, n + 1)
                nc.vector.tensor_tensor(quad(K.qkd[:, t, :, :]), quad(dec_of(t)),
                                        wide(key_bank(t)[:, 256:512].rearrange("p (j c) -> p j c", c=128), 1, 2),
                                        ALU.mult).then_inc(S.qkd_ready, 1)

        def setup_d(t):
            n = TILES * G + t
            dve.wait_ge(S.bd_ready, n + 1)
            dve.wait_ge(S.kk_ready, n + 1)
            nc.vector.tensor_tensor(quad(K.bt[t][:, :, :]), quad(dec_of(t)),
                                    wide(key_bank(t)[:, 0:256].rearrange("p (j c) -> p j c", c=128), 1, 2),
                                    ALU.mult).then_inc(S.bt_ready, 1)
            dve.wait_ge(S.bt_ready, n + 1 + CREDIT)
            nc.vector.tensor_tensor(quad(K.e[:, t, :, :]), quad(K.bt[t][:, :, :]), wide(K.level[0][:, :, :], 2, 2),
                                    ALU.mult).then_inc(S.e0_ready, 1)
            dve.wait_ge(S.e0_ready, n + 1)
            nc.vector.tensor_tensor(K.e[:, t, :, :], wide(K.ident[:, :], 1, 4), K.e[:, t, :, :], ALU.subtract)\
                .then_inc(S.es_ready, 1)
        for step in (setup_a, setup_b, setup_c, setup_d):
            for t in range(3):
                step(t)
        for hb in range(2):
            for l in range(1, LEVELS):
                for i in range(3):
                    t = 3 * hb + i
                    c = 36 * G + 18 * hb + 3 * (l - 1) + i
                    dve.wait_ge(S.w_ready, c + 1 + CREDIT)
                    nc.vector.tensor_tensor(K.e[:, t, :, :], K.e[:, t, :, :],
                                            pb[2 + c_par(l, i)][:, :].rearrange("p (c v) -> p c v", v=128),
                                            ALU.subtract).then_inc(S.e_ready, 1)
                    if hb == 0:
                        late = 3 + (l - 1) // 2
                        if i == 0:
                            (setup_a, setup_c)[(l - 1) % 2](late)
                        if i == 2:
                            (setup_b, setup_d)[(l - 1) % 2](late)

    def dve_scan(dve, G, project):
        s = DN_SLAB + 6 * (G + 1)
        for n, (f, b, x) in enumerate(scan_steps()):
            a = TILES * G + n
            ops = conv_ops(dve, G + 1, n - 1) if project and n > 0 else iter(())
            dve.wait_ge(S.sk_ready, a + 1)
            for d, t in enumerate((f, b)):
                for j in range(2):
                    c = 2 * d + j
                    nc.vector.scalar_tensor_tensor(out=K.rr[:, c, :], in0=pb[4][:, 128 * c:128 * c + 128],
                                                   scalar=K.negeg[:, t, bass.ds(8 * d + 2 * G + j, 1)], in1=K.vs[:, t, j, :],
                                                   op0=ALU.mult, op1=ALU.add).then_inc(S.rr_ready, 1)
            if project and n > 0:
                split_lo(dve, s + n + 1, (n - 1) % 2, 1024)
            take(ops, 2)
            dve.wait_ge(S.sx_ready, a + 1)
            for d, t in enumerate((f, b)):
                nc.vector.tensor_tensor(K.vn[:, 2 * d:2 * d + 2, :],
                                        pb[5][:, 256 * d:256 * d + 256].rearrange("p (j v) -> p j v", v=128),
                                        wide(K.beta[:, t, bass.ds(8 * d + 2 * G, 2)], 2, 128), ALU.mult).then_inc(S.vn_ready, 1)
            take(ops, 3)
            dve.wait_ge(S.se_ready, a + 1)
            dve.wait_ge(S.su_ready, a + 1)
            nc.vector.tensor_tensor(K.st[:, :, :], K.st[:, :, :], pb[6][:, :].rearrange("p (c v) -> p c v", v=128), ALU.add)\
                .then_inc(S.st_ready, 1)
            if x is not None:
                dve.wait_ge(S.so_ready, 4 * G + x + 1)
                for d, t in enumerate((f, b)):
                    out = K.ot[:, bass.ds(2 * G, 2), 128 * t:128 * t + 128]
                    src = pb[7][:, 256 * d:256 * d + 256].rearrange("p (j c) -> p j c", c=128)
                    if x < 2:
                        nc.vector.tensor_copy(out, src).then_inc(S.ot_ready, 1)
                    else:
                        dve.wait_ge(S.ot_ready, 8 * G + 4)
                        nc.vector.tensor_tensor(out, out, src, ALU.add).then_inc(S.ot_ready, 1)
            take(ops, 99)
        if project:
            split_lo(dve, s + 7, 1, 1024)
            take(conv_ops(dve, G + 1, 5), 99)

    def dve_tail(dve):
        n = 0
        for i, (kind, m) in enumerate(TAIL):
            split_lo(dve, TAIL_SLAB + i + 2, i % 2, 1024)
            if kind == "u":
                dve.wait_ge(S.ostd_ready, m + 1)
                nc.vector.reciprocal(pb[5][:, :], pb[5][:, :]).then_inc(S.orstd_ready, 1)
                dve.wait_ge(S.orstd_ready, m + 1)
                nc.vector.scalar_tensor_tensor(out=K.ot[:, m, :], in0=K.ot[:, m, :], scalar=K.dngain[:, 0:1],
                                               in1=pb[5][:, :], op0=ALU.mult, op1=ALU.mult).then_inc(S.on_ready, 1)
            elif kind in "zp":
                dve.wait_ge(S.evac, TAIL_EVIC + i + 1 + CREDIT)
                if kind == "z":
                    dve.wait_ge(S.on_ready, m + 1)
                    if n > 0:
                        dve.wait_ge(S.y_ready, n)
                    src, dst = K.ot[:, m, :], K.ytmp[:, :]
                else:
                    src = dst = K.ypre[:, m % 4, :]
                nc.vector.tensor_tensor(dst, src, K.zs[:, :], ALU.mult).then_inc(S.zs_used, 1)
                n += 1
                y = m + 8 * (kind == "p")
                dve.wait_ge(S.yh_ready, n)
                nc.vector.tensor_tensor(K.yl[y][:, :], dst, K.yh[y][:, :].bitcast(F32), ALU.subtract).then_inc(S.y_ready, 1)
            if i in SPLIT_AT:
                m = SPLIT_AT[i]
                dve.wait_ge(S.dh_ready, m + 1)
                nc.vector.tensor_tensor(K.dl[:, m % 4, :], K.box[:, :, :].rearrange("p r c -> p (r c)"),
                                        K.dh[:, m % 4, :].bitcast(F32), ALU.subtract).then_inc(S.d_ready, 1)
        for m in range(8):
            split_lo(dve, OUT_SLAB + 2 * m + 2, 0, 1024)
            dve.wait_ge(S.slab_done, OUT_SLAB + 2 * m + 2 + CREDIT)
            nc.vector.scalar_tensor_tensor(out=h[:, m, :], in0=pb[m % 2][:, :], scalar=K.modv[:, 16 + m, 0:1],
                                           in1=h[:, m, :], op0=ALU.mult, op1=ALU.add).then_inc(S.res_ready, 1)
            split_lo(dve, OUT_SLAB + 2 * m + 3, 1, 1024)
        dve.wait_ge(S.fstd_ready, 1)
        nc.vector.reciprocal(K.rstd[:, :], K.std[:, :]).then_inc(S.frstd_ready, 1)
        dve.wait_ge(S.frstd_ready, 1)
        for m in range(8):
            nc.vector.scalar_tensor_tensor(out=h[:, m, :], in0=h[:, m, :], scalar=K.fgain[:, m:m + 1], in1=K.rstd[:, :],
                                           op0=ALU.mult, op1=ALU.mult).then_inc(S.evac, 1)
        for m in range(8):
            dve.wait_ge(S.xgh_ready, m + 1)
            nc.vector.scalar_tensor_tensor(out=K.xgl[:, m, :], in0=h[:, m, :], scalar=K.gains[:, m:m + 1],
                                           in1=K.xgh[:, m, :].bitcast(F32), op0=ALU.mult, op1=ALU.subtract)\
                .then_inc(S.xg_ready, 1)

    def dve_prog(dve):
        K.convchain = Chain(dve, S.short_step)
        K.gatechain = Chain(dve, S.gate_step)
        dve_start(dve)
        for i in range(6):
            split_lo(dve, DN_SLAB + i + 2, i % 2, 1024)
            take(conv_ops(dve, 0, i), 99)
            if i == 1:
                dve_gates(dve)
            if i == 3:
                dve_sums(dve)
        with dve.Fori(0, GROUPS - 1) as G:
            dve_solve(dve, G)
            dve_scan(dve, G, True)
        dve_solve(dve, GROUPS - 1)
        dve_scan(dve, GROUPS - 1, False)
        dve_tail(dve)

    def pe_start(pe):
        pe.wait_ge(S.cond_ready, 1)

        def modulate(lo, hi, bank, base):
            with pe.Fori(lo, hi) as i:
                for slot in range(2):
                    pe.wait_ge(S.raw_full[slot], 16 * i + 16)
                    for k in range(8):
                        last = nc.tensor.matmul(bank[:, bass.ds(4 * i + (2 * slot - base), 2)],
                                                K.raw[:, slot, 128 * k:128 * k + 128],
                                                K.cvec[:, k, :], start=(k == 0), stop=(k == 7))
                    last.then_inc(S.raw_read, 1)
        modulate(0, 4, pb[7], 0)
        pe.wait_ge(S.ssum, 16)
        nc.tensor.matmul(pb[4][:, :], K.ones[:, :], K.sacc[:, 0:TOK], start=True, stop=True).then_inc(S.sss_ready, 1)
        nc.tensor.matmul(pb[5][:, 0:CTX], K.ones[:, :], K.sacc[:, TOK:ALLT], start=True, stop=True).then_inc(S.sss_ready, 1)
        modulate(4, 8, pb[7], 0)
        modulate(8, MOD_SLABS // 2, pb[3], 32)

    def pe_gates(pe):
        pe.wait_ge(S.wab_ready, 1)
        pe.wait_ge(S.hn_ready, 16)
        for t in range(TILES):
            for k in range(8):
                for n, (a, b) in enumerate(((hnh, K.wabh), (hnh, K.wabl), (hnl, K.wabh))):
                    last = nc.tensor.matmul(pb[6][:, 32 * t:32 * t + 32], a[:, k, 128 * t:128 * t + 128], b[:, k, :],
                                            start=(k == 0 and n == 0), stop=(k == 7 and n == 2))
        last.then_inc(S.ab_ready, 1)

    def pe_sums(pe):
        pe.wait_ge(S.lg_ready, 1)
        for d in range(2):
            nc.tensor.matmul(pb[7][:, 0:96].rearrange("p (t c) -> p t c", c=16)[:, :, 8 * d:8 * d + 8], K.incl[d][:, :],
                             K.logd[:, :, 8 * d:8 * d + 8], start=True, stop=True)
        nc.tensor.matmul(pb[7][:, 96:192], K.ones[:, :], K.logd[:, :, :].rearrange("p t c -> p (t c)"), start=True, stop=True)\
            .then_inc(S.cums_ready, 1)

    def pe_slab(pe, s, v, slot, ctx, first=False):
        for part in slab_parts(pe, s, v, slot, ctx, first):
            pass

    def slab_parts(pe, s, v, slot, ctx, first=False):
        pe.wait_ge(S.raw_read, s + 1 + CREDIT)
        pe.wait_ge(S.evac, v + 1)
        for k in range(8):
            if first:
                pe.wait_ge(S.hn_ready, 2 * k + 2)
            last = mm3(pb[slot][:, :], slot, k, hnh[:, k, 0:TOK], hnl[:, k, 0:TOK], k == 0, k == 7)
            if k in (2, 4):
                yield
        if ctx:
            for k in range(8):
                last = mm3(pb[2 + slot][:, 0:CTX], slot, k, hnh[:, k, TOK:ALLT], hnl[:, k, TOK:ALLT], k == 0, k == 7)
        last.then_inc(S.slab_done, 1)
        yield

    def pe_project(pe, G):
        for i in range(6):
            if i == 1:
                pe.wait_ge(S.mod_ready, 4)
            pe_slab(pe, DN_SLAB + 6 * G + i, DN_EVIC + 6 * G + i, i % 2, HEAD_SLABS[i][0] > 0, first=i == 0)
            if i == 1:
                pe_gates(pe)
            if i == 3:
                pe_sums(pe)

    def pe_solve(pe, G):
        pe.wait_ge(S.evac, DN_EVIC + 6 * G + 6 + CREDIT)
        pe.wait_ge(S.head_ready, 6 * G + 6 + CREDIT)

        def turn_keys(t):
            n = TILES * G + t
            w = 4 if t < 4 else 2
            pe.wait_ge(S.kqn_ready, n - 1 + CREDIT)
            lo = 128 * t
            for c in range(w):
                src = K.hv[HEAD_SLABS.index(((1, 0), (1, 1), (0, 0), (0, 1))[c])]
                last = nc.tensor.transpose(pb[t % 2][:, 128 * c:128 * c + 128], src[:, lo:lo + 128], K.ident[:, :])
            last.then_inc(S.tk_ready, 1)
            pe.wait_ge(S.vs_ready, n - 1 + CREDIT)
            for j in range(2):
                last = nc.tensor.transpose(pb[2 + t % 2][:, 128 * j:128 * j + 128], K.hv[HEAD_SLABS.index((2, j))][:, lo:lo + 128], K.ident[:, :])
            last.then_inc(S.tv_ready, 1)

        def turn_back(t):
            n = TILES * G + t
            w = 4 if t < 4 else 2
            pe.wait_ge(S.kqn_ready, n + 1 + CREDIT)
            pe.wait_ge(S.kq_ready, n - 1 + CREDIT)
            for c in range(w):
                last = nc.tensor.transpose(pb[4 + t % 2][:, 128 * c:128 * c + 128], K.kqn[t % 2][:, c, :], K.ident[:, :])
            last.then_inc(S.kb_ready, 1)
        turn_keys(0)
        for t in range(1, TILES):
            turn_keys(t)
            turn_back(t - 1)
        turn_back(TILES - 1)
        pe.wait_ge(S.kq_ready, TILES * G + TILES + CREDIT)

        def setup(t):
            n = TILES * G + t
            pe.wait_ge(S.dg_ready, n + 1)
            if t > 2:
                pe.wait_ge(S.eg_ready, 4 * G + min(t, 4))
                pe.wait_ge(S.bt_ready, n + CREDIT)
            nc.tensor.matmul(sum_bank(t)[:, :], K.ones[:, :], dg_of(t).rearrange("p c v -> p (c v)"), start=True, stop=True)\
                .then_inc(S.gb_ready, 1)
            for j in range(2):
                last = nc.tensor.matmul(key_bank(t)[:, 128 * j:128 * j + 128], K.kq[:, t, j, :], K.kq[:, t, j, :],
                                        start=True, stop=True)
                if t < 4:
                    last = nc.tensor.matmul(key_bank(t)[:, 256 + 128 * j:384 + 128 * j], K.kq[:, t, j, :], K.kq[:, t, 2 + j, :],
                                            start=True, stop=True)
            last.then_inc(S.kk_ready, 1)
        pe.wait_ge(S.vs_ready, TILES * G + TILES + CREDIT)
        for i in range(3):
            setup(i)
        for i in range(3):
            pe.wait_ge(S.es_ready, TILES * G + i + 1)
            turn_inverse(pe, G, 0, 0, i)
        for hb in range(2):
            if hb == 1:
                pe.wait_ge(S.es_ready, TILES * G + TILES)
                for i in range(3):
                    turn_inverse(pe, G, 1, 0, i)
            for l in range(1, LEVELS):
                for i in range(3):
                    c = 36 * G + 18 * hb + 3 * (l - 1) + i
                    par = c_par(l, i)
                    pe.wait_ge(S.bl_ready, c + 1 + CREDIT)
                    pe.wait_ge(S.dd_ready, c + 1 + CREDIT)
                    pe.wait_ge(S.pp_ready, c - 1 + CREDIT)
                    for q in range(4):
                        last = nc.tensor.matmul(pb[par][:, 128 * q:128 * q + 128], K.bl[:, par, q, :], K.dd[:, i, q, :],
                                                start=True, stop=True)
                    last.then_inc(S.p_ready, 1)
                for i in range(3):
                    t = 3 * hb + i
                    c = 36 * G + 18 * hb + 3 * (l - 1) + i
                    par = c_par(l, i)
                    pe.wait_ge(S.pp_ready, c + 1 + CREDIT)
                    pe.wait_ge(S.e_ready, c - 1 + CREDIT)
                    for q in range(4):
                        last = nc.tensor.matmul(pb[2 + par][:, 128 * q:128 * q + 128], K.pp[:, par, q, :], K.e[:, t, q, :],
                                                start=True, stop=True)
                    last.then_inc(S.w_ready, 1)
                if hb == 0 and l % 2 == 1:
                    setup(3 + l // 2)
                if l < LEVELS - 1:
                    for i in range(3):
                        pe.wait_ge(S.e_ready, 36 * G + 18 * hb + 3 * (l - 1) + i + 1 + CREDIT)
                        turn_inverse(pe, G, hb, l, i)

    def pe_scan(pe, G, project):
        pe.wait_ge(S.e_ready, 36 * G + 36 + CREDIT)
        pe.wait_ge(S.ks_ready, TILES * G + TILES + CREDIT)
        pe.wait_ge(S.vs_ready, TILES * G + TILES + CREDIT)
        pe.wait_ge(S.qkd_ready, 4 * G + 4)
        pe.wait_ge(S.qd_ready, 4 * G + 4 + CREDIT)
        for n, (f, b, x) in enumerate(scan_steps()):
            a = TILES * G + n
            order = [(t, j, 2 * d + j) for d, t in enumerate((f, b)) for j in range(2)]

            def part(c):
                return slice(128 * c, 128 * c + 128)
            parts = slab_parts(pe, DN_SLAB + 6 * (G + 1) + n, DN_EVIC + 6 * (G + 1) + n, n % 2, HEAD_SLABS[n][0] > 0) \
                if project else iter(())
            pe.wait_ge(S.st_ready, a + G + 1)
            for t, j, c in order:
                last = nc.tensor.matmul(pb[4][:, part(c)], K.kq[:, t, j, :], K.st[:, c, :], start=True, stop=True)
            last.then_inc(S.sk_ready, 1)
            if x is not None:
                if x > 0:
                    pe.wait_ge(S.ot_ready, 8 * G + 2 * x)
                for t, j, c in order:
                    last = nc.tensor.matmul(pb[7][:, part(c)], K.st[:, c, :], K.qd[:, t, c, :], start=(c == 0), stop=False)
                last.then_inc(S.sd_used, 1)
            next(parts, None)
            for t, j, c in order:
                pe.wait_ge(S.rr_ready, 4 * a + c + 1)
                last = nc.tensor.matmul(pb[5][:, part(c)], K.e[:, t, c, :], K.rr[:, c, :], start=True, stop=True)
            last.then_inc(S.sx_ready, 1)
            next(parts, None)
            for t, j, c in order:
                pe.wait_ge(S.vn_ready, 2 * a + c // 2 + 1)
                last = nc.tensor.matmul(pb[6][:, part(c)], K.ks[:, t, c, :], K.vn[:, c, :], start=True, stop=True)
            last.then_inc(S.su_ready, 1)
            if x is not None:
                for t, j, c in order:
                    last = nc.tensor.matmul(pb[7][:, part(c)], K.vn[:, c, :], K.qkd[:, t, c, :], start=False, stop=(c == 3))
                last.then_inc(S.so_ready, 1)
            next(parts, None)
        pe.wait_ge(S.st_ready, 7 * G + 7)
        pe.wait_ge(S.ot_ready, 8 * G + 8)

    def turn_inverse(pe, G, hb, l, i):
        pe.wait_ge(S.dd_ready, 36 * G + 18 * hb + 3 * l + i - 1 + CREDIT)
        for q in range(4):
            last = nc.tensor.transpose(pb[6 + turn_par(l, i)][:, 128 * q:128 * q + 128], K.e[:, 3 * hb + i, q, :], K.ident[:, :])
        last.then_inc(S.tt_ready, 1)

    def pe_tail(pe):
        for i, (kind, m) in enumerate(TAIL):
            a, b = TAIL_SLAB + i, TAIL_EVIC + i
            slot = a % 2
            if kind == "w":
                pe.wait_ge(S.raw_read, a + 1 + CREDIT)
                pe.wait_ge(S.evac, b + 1)
                pe.wait_ge(S.d_ready, 4 * m + 4)
                for g2 in range(2):
                    for e in range(2):
                        for k in range(2):
                            last = mm3(pb[(2, 3, 6, 7)[2 * g2 + e]][:, :], slot, 4 * g2 + 2 * e + k,
                                       K.dh[:, 2 * g2 + k, :], K.dl[:, 2 * g2 + k, :], k == 0, k == 1)
                last.then_inc(S.slab_done, 1)
            else:
                pe_slab(pe, a, b, slot, False)
            if kind == "u":
                pe.wait_ge(S.osq_ready, m + 1)
                if m > 0:
                    pe.wait_ge(S.on_ready, m)
                nc.tensor.matmul(pb[5][:, :], K.ones[:, :], K.os[:, :], start=True, stop=True).then_inc(S.oss_ready, 1)
        for m in range(8):
            a = OUT_SLAB + 2 * m
            if m == 0:
                pe.wait_ge(S.evac, OUT_EVIC + CREDIT)
            if m >= 2:
                pe.wait_ge(S.res_ready, m - 1)
            for half in range(2):
                pe.wait_ge(S.raw_read, a + half + 1 + CREDIT)
                for j in range(8):
                    k = OUT_ORDER[8 * half + j]
                    if m == 0:
                        pe.wait_ge(S.y_ready, 8 * half + j + 1)
                    last = mm3(pb[m % 2][:, :], half, j, K.yh[k][:, :], K.yl[k][:, :], half == 0 and j == 0, half == 1 and j == 7)
                last.then_inc(S.slab_done, 1)

    def pe_final(pe):
        pe.wait_ge(S.fsq_step, 17)
        nc.tensor.matmul(pb[7][:, :], K.ones[:, :], K.sqsum[:, :], start=True, stop=True).then_inc(S.fss_ready, 1)

    def pe_prog(pe):
        pe_start(pe)
        pe_project(pe, 0)
        with pe.Fori(0, GROUPS - 1) as G:
            pe_solve(pe, G)
            pe_scan(pe, G, True)
        pe_solve(pe, GROUPS - 1)
        pe_scan(pe, GROUPS - 1, False)
        pe_tail(pe)
        pe_final(pe)

    def pool_group(pool, G):
        def quad(x):
            return x.rearrange("p (d j) c -> p d j c", j=2)
        for t in range(TILES):
            n = TILES * G + t
            pool.wait_ge(S.kqn_ready, n + 1 + CREDIT)
            nc.gpsimd.tensor_tensor(quad(K.ks[:, t, :, :]), wide(K.kqn[t % 2][:, 0:2, :], 1, 2),
                                    wide(heads(K.tail_s[:, t, :], G), 3, 128), ALU.mult).then_inc(S.ks_ready, 1)

        def setup(t):
            n = TILES * G + t
            pool.wait_ge(S.decm_ready, 2 * n + 2)
            pool.wait_ge(S.qkd_ready, 4 * G + min(t + 1, 4))
            nc.gpsimd.tensor_tensor(quad(dec_of(t)), quad(dec_of(t)),
                                    wide(heads(K.beta[:, t, :], G), 3, 128), ALU.mult).then_inc(S.bd_ready, 1)

        def setup_q(t):
            if t < 4:
                pool.wait_ge(S.eg_ready, 4 * G + t + 1)
                nc.gpsimd.tensor_tensor(quad(K.qd[:, t, :, :]), quad(dg_of(t)),
                                        wide(K.kq[:, t, 2:4, :], 1, 2), ALU.mult).then_inc(S.qd_ready, 1)
        for i in range(3):
            setup(i)
        for i in range(3):
            setup_q(i)
        for hb in range(2):
            for l in range(1, LEVELS):
                for i in range(3):
                    c = 36 * G + 18 * hb + 3 * (l - 1) + i
                    pool.wait_ge(S.bt_ready, TILES * G + 3 * hb + 3 + CREDIT)
                    pool.wait_ge(S.p_ready, c - 1 + CREDIT)
                    nc.gpsimd.tensor_tensor(quad(K.bl[:, c_par(l, i), :, :]), quad(K.bt[3 * hb + i][:, :, :]),
                                            wide(K.level[l][:, :, :], 2, 2), ALU.mult).then_inc(S.bl_ready, 1)
                    if hb == 0 and ((l in (3, 5) and i == 0) or (l == LEVELS - 1 and i == 2)):
                        setup(3 + (l - 2) // 2)
                        setup_q(3 + (l - 2) // 2)
        pool.wait_ge(S.e_ready, 36 * G + 36 + CREDIT)
        hold(pool, S)
        nc.gpsimd.memset(K.st[:, :, :], 0.0).then_inc(S.st_ready, 1)
        for n, (f, b, x) in enumerate(scan_steps()):
            a = TILES * G + n
            if x is None:
                pool.wait_ge(S.sk_ready, a + 1)
            else:
                pool.wait_ge(S.sd_used, 4 * G + x + 1)
            for d, t in enumerate((f, b)):
                ins = nc.gpsimd.tensor_tensor(K.st[:, 2 * d:2 * d + 2, :], K.st[:, 2 * d:2 * d + 2, :],
                                              wide(K.etot[:, t, bass.ds(8 * d + 2 * G, 2)], 2, 128), ALU.mult)
            ins.then_inc(S.se_ready, 1)

    def pool_tail(pool):
        for grid in K.upad:
            nc.gpsimd.memset(grid[:, :, :], 0.0).then_inc(S.pad_step, 1)
        ch = K.poolchain
        pool.wait_ge(S.pad_step, 3)
        for m in range(8):
            if m % 2 == 0:
                if m > 0:
                    pool.wait_ge(S.pooled, m)
                pool.dma_start(K.icnt[:, :], K.c_icnt[m // 2, :, :]).then_inc(S.icnt_in, 16)
            w = WINDOWS[m // 2]
            pool.wait_ge(S.evac, TAIL_EVIC + TAIL.index(("u", m)) + 1 + CREDIT)
            src, dst, k = K.upad[0], K.upad[1], 1
            while k < w:
                n = PADW - 2 * k + 1
                ch.link(nc.gpsimd.tensor_tensor(dst[:, :, 0:n], src[:, :, 0:n], src[:, :, k:k + n], ALU.add))
                src, dst = dst, (K.upad[2] if dst is K.upad[1] else K.upad[1])
                k *= 2
            col = src[:, :, 8 - w // 2:8 - w // 2 + GRID_W]
            if m > 0:
                pool.wait_ge(S.d_ready, m)
            if w < 16:
                ch.link(nc.gpsimd.tensor_copy(K.box[:, :, :], col))
                for sft in range(-(w // 2), w - w // 2):
                    if sft == 0:
                        continue
                    lo, hi = max(0, -sft), min(GRID_H, GRID_H - sft)
                    ch.link(nc.gpsimd.tensor_tensor(K.box[:, lo:hi, :], K.box[:, lo:hi, :], col[:, lo + sft:hi + sft, :], ALU.add))
            else:
                ch.link(nc.gpsimd.tensor_tensor(K.box[:, 0:4, :], col[:, 0:4, :], col[:, 4:8, :], ALU.add))
                ch.link(nc.gpsimd.tensor_tensor(K.box[:, 0:2, :], K.box[:, 0:2, :], K.box[:, 2:4, :], ALU.add))
                ch.link(nc.gpsimd.tensor_tensor(dst[:, 0, 0:GRID_W], K.box[:, 0, :], K.box[:, 1, :], ALU.add))
                ch.link(nc.gpsimd.tensor_copy(K.box[:, :, :], wide(dst[:, 0, 0:GRID_W], 1, GRID_H)))
            pool.wait_ge(S.icnt_in, 16 * (m // 2 + 1))
            ch.link(nc.gpsimd.tensor_tensor(K.box[:, :, :], K.box[:, :, :], K.icnt[:, :].rearrange("p (r c) -> p r c", c=GRID_W), ALU.mult))
            nc.gpsimd.tensor_tensor(K.box[:, :, :], K.box[:, :, :], K.upad[0][:, :, 8:8 + GRID_W], ALU.subtract).then_inc(S.pooled, 1)

    def pool_prog(pool):
        K.poolchain = Chain(pool, S.box_step)
        with pool.Fori(0, GROUPS) as G:
            pool_group(pool, G)
        pool.wait_ge(S.st_ready, 7 * GROUPS)
        pool.wait_ge(S.ot_ready, 8 * GROUPS)
        pool_tail(pool)
        fsq = Chain(pool, S.fsq_step)
        pool.wait_ge(S.res_ready, 1)
        fsq.link(nc.gpsimd.memset(K.sqsum[:, :], 0.0))
        for m in range(8):
            pool.wait_ge(S.res_ready, m + 1)
            fsq.link(nc.gpsimd.tensor_tensor(K.sqtmp[:, :], h[:, m, :], h[:, m, :], ALU.mult))
            fsq.link(nc.gpsimd.tensor_tensor(K.sqsum[:, :], K.sqsum[:, :], K.sqtmp[:, :], ALU.add))
        pool.wait_ge(S.fss_ready, 1)
        K.pool_square_first(pool)

    return sp_prog, act_prog, dve_prog, pe_prog, pool_prog

def transformer_layers(K):
    nc, S = K.nc, K.S
    pb, h, xgh, xgl, rstd = K.pb, K.h, K.xgh, K.xgl, K.rstd
    split_hi, split_lo, mm3 = K.split_hi, K.split_lo, K.mm3

    def norm_index(l, n):
        return 4 * l + n

    def act_gain(act, q, m, v):
        act.wait_ge(S.evac, v + 3)
        nc.scalar.activation(xgh[:, m, :], h[:, m, :], ACT.Copy,
                             scale=K.gains[:, bass.ds(8 * q + m, 1)]).then_inc(S.xgh_ready, 1)

    def dve_gain(dve, q, m):
        dve.wait_ge(S.xgh_ready, 8 * q + m + 1)
        nc.vector.scalar_tensor_tensor(out=xgl[:, m, :], in0=h[:, m, :],
                                       scalar=K.gains[:, bass.ds(8 * q + m, 1)],
                                       in1=xgh[:, m, :].bitcast(F32), op0=ALU.mult,
                                       op1=ALU.subtract).then_inc(S.xg_ready, 1)

    def pool_square(pool, q, m, v, first=False):
        if first:
            if first != "start":
                pool.wait_ge(S.ss_ready, q)
            hold(pool, S)
            nc.gpsimd.memset(K.sqsum[:, :], 0.0).then_inc(S.sq_zeroed, 1)
            pool.wait_ge(S.sq_zeroed, q + 1)
        pool.wait_ge(S.evac, v + 3)
        pool.wait_ge(S.sq_added, 8 * q + m + CREDIT)
        nc.gpsimd.tensor_tensor(K.sqtmp[:, :], h[:, m, :], h[:, m, :], ALU.mult).then_inc(S.sq_made, 1)
        pool.wait_ge(S.sq_made, 8 * q + m + 1)
        nc.gpsimd.tensor_tensor(K.sqsum[:, :], K.sqsum[:, :], K.sqtmp[:, :], ALU.add).then_inc(S.sq_added, 1)

    def pe_sum_squares(pe, q):
        pe.wait_ge(S.sq_added, 8 * (q + 1) + CREDIT)
        pe.wait_ge(S.rstd_ready, q + CREDIT)
        nc.tensor.matmul(pb[7][:, :], K.ones[:, :], K.sqsum[:, :], start=True, stop=True)\
            .then_inc(S.ss_ready, 1)

    def act_std(act, q):
        act.wait_ge(S.ss_ready, q + 1)
        act.wait_ge(S.rstd_ready, q + CREDIT)
        nc.scalar.activation(K.std[:, :], pb[7][:, :], ACT.Sqrt, bias=K.eps[:, 0:1],
                             scale=1.0 / D).then_inc(S.std_ready, 1)

    def dve_rstd(dve, q, v):
        dve.wait_ge(S.std_ready, q + 1 + CREDIT)
        dve.wait_ge(S.evac, v + 2)
        nc.vector.reciprocal(rstd[:, :], K.std[:, :]).then_inc(S.rstd_ready, 1)
        dve.wait_ge(S.rstd_ready, q + 1 + CREDIT)

    def pe_project(pe, s, v, slot, q=None):
        pe.wait_ge(S.raw_read, s + 1 + CREDIT)
        pe.wait_ge(S.evac, v + 1)
        for k in range(8):
            if q is not None:
                pe.wait_ge(S.xg_ready, 8 * q + k + 1)
            last = mm3(pb[slot][:, :], slot, k, xgh[:, k, :], xgl[:, k, :], k == 0, k == 7)
        last.then_inc(S.slab_done, 1)

    def first_squares(pool):
        for m in range(8):
            pool_square(pool, 0, m, K.layer_evic - 8 + m, first="start" if m == 0 else None)
    K.pool_square_first = first_squares

    hid_h, hid_l = K.hid_h, K.hid_l

    def ff_pe(pe, l, w):
        q = norm_index(l, 2 * w)
        f = 2 * l + w
        s0, v0 = K.slab(l, ("ff1in", "ff2in")[w]), K.evic(l, ("ff1in", "ff2in")[w])

        def pair(i, first):
            for slot in range(2):
                pe_project(pe, s0 + 2 * i + slot, v0 + 2 * i + slot, slot, q if first and slot == 0 else None)
                if first and slot == 0:
                    pe_sum_squares(pe, q)
        pair(0, True)
        with pe.Fori(1, FT) as i:
            pair(i, False)
        s1, v1 = K.slab(l, ("ff1out", "ff2out")[w]), K.evic(l, ("ff1out", "ff2out")[w])

        def out_tile(m, par, first):
            pe.wait_ge(S.evac, v1 + m + 1)
            for half in range(2):
                pe.wait_ge(S.raw_read, s1 + 2 * m + half + 1 + CREDIT)
                for j in range(11):
                    k = 11 * half + j
                    if first and k >= FT - 3:
                        pe.wait_ge(S.hid_ready, FT * f + k + 1 + CREDIT)
                    last = mm3(pb[par][:, :], half, j, hid_h[:, k, :], hid_l[:, k, :], k == 0, k == FT - 1)
                last.then_inc(S.slab_done, 1)
        out_tile(0, 0, True)
        out_tile(1, 1, False)
        with pe.Fori(1, 4) as i:
            for par in range(2):
                out_tile(2 * i + par, par, False)

    def ff_act(act, l, w):
        q = norm_index(l, 2 * w)
        f = 2 * l + w
        s0, v0 = K.slab(l, ("ff1in", "ff2in")[w]), K.evic(l, ("ff1in", "ff2in")[w])
        s1, v1 = K.slab(l, ("ff1out", "ff2out")[w]), K.evic(l, ("ff1out", "ff2out")[w])

        def pair(i, first, cols):
            n = FT * f + i
            split_hi(act, s0 + 2 * i + 2, 0, cols)
            if first:
                act_std(act, q)
            act.wait_ge(S.evac, v0 + 2 * i + 3)
            act.wait_ge(S.g_ready, n + CREDIT)
            nc.scalar.activation(K.silu[:, :], K.t1[:, :], ACT.Silu).then_inc(S.silu_ready, 1)
            split_hi(act, s0 + 2 * i + 3, 1, cols)
            act.wait_ge(S.g_ready, n + 1 + CREDIT)
            nc.scalar.activation(hid_h[:, i, :], K.g[:, :], ACT.Copy).then_inc(S.hidh_ready, 1)
        pair(0, True, 1024)
        with act.Fori(1, FT - 1) as i:
            pair(i, False, 1024)
        pair(FT - 1, False, 1408)

        (forget_act, embed_act)[w](act, l)

        def out_tile(m, cols):
            split_hi(act, s1 + 2 * m + 2, 0, cols)
            act_gain(act, q + 1, m, v1 + m)
            split_hi(act, s1 + 2 * m + 3, 1, cols)
        with act.Fori(0, 7) as m:
            out_tile(m, 1408)
        out_tile(7, 1024 if w == 0 else 1280)

    def ff_dve(dve, l, w):
        q = norm_index(l, 2 * w)
        f = 2 * l + w
        s0, v0 = K.slab(l, ("ff1in", "ff2in")[w]), K.evic(l, ("ff1in", "ff2in")[w])
        s1, v1 = K.slab(l, ("ff1out", "ff2out")[w]), K.evic(l, ("ff1out", "ff2out")[w])

        def pair(i, first, cols):
            n = FT * f + i
            split_lo(dve, s0 + 2 * i + 2, 0, cols)
            if first:
                dve_rstd(dve, q, v0)
            dve.wait_ge(S.silu_ready, n + CREDIT)
            nc.vector.tensor_tensor(K.t1[:, :], pb[0][:, :], rstd[:, :], ALU.mult).then_inc(S.evac, 1)
            split_lo(dve, s0 + 2 * i + 3, 1, cols)
            dve.wait_ge(S.g_ready, n + CREDIT)
            nc.vector.tensor_tensor(K.t2[:, :], pb[1][:, :], rstd[:, :], ALU.mult).then_inc(S.evac, 1)
            dve.wait_ge(S.hidh_ready, n + 1)
            nc.vector.tensor_tensor(hid_l[:, i, :], K.g[:, :], hid_h[:, i, :].bitcast(F32),
                                    ALU.subtract).then_inc(S.hid_ready, 1)
        pair(0, True, 1024)
        with dve.Fori(1, FT - 1) as i:
            pair(i, False, 1024)
        pair(FT - 1, False, 1408)

        (forget_dve, embed_dve)[w](dve, l)

        def out_tile(m, par, cols):
            split_lo(dve, s1 + 2 * m + 2, 0, cols)
            dve.wait_ge(S.slab_done, s1 + 2 * m + 2 + CREDIT)
            nc.vector.scalar_tensor_tensor(out=h[:, m, :], in0=pb[par][:, :], scalar=FFN_RES,
                                           in1=h[:, m, :], op0=ALU.mult, op1=ALU.add).then_inc(S.evac, 1)
            dve_gain(dve, q + 1, m)
            split_lo(dve, s1 + 2 * m + 3, 1, cols)
        with dve.Fori(0, 3) as i:
            for par in range(2):
                out_tile(2 * i + par, par, 1408)
        out_tile(6, 0, 1408)
        out_tile(7, 1, 1024 if w == 0 else 1280)

    def forget_pool(pool, l):
        pool.wait_ge(S.slab_done, K.slab(l, "ff1in") + 2)
        hold(pool, S)
        nc.gpsimd.memset(K.wf_h[:, :, :].bitcast(F32), 0.0).then_inc(S.wf_zero, 1)
        nc.gpsimd.memset(K.wf_l[:, :, :].bitcast(F32), 0.0).then_inc(S.wf_zero, 1)

    def forget_act(act, l):
        act.wait_ge(S.wf_zero, 2 * l + 2)
        act.wait_ge(S.wf_raw, 16 * (l + 1))
        nc.scalar.activation(K.wf_h[:, :, 0:8], K.wf[:, :, :], ACT.Copy).then_inc(S.wfh_ready, 1)

    def forget_dve(dve, l):
        dve.wait_ge(S.wf_zero, 2 * l + 2)
        dve.wait_ge(S.wfh_ready, l + 1)
        nc.vector.tensor_tensor(K.wf_l[:, :, 0:8], K.wf[:, :, :], K.wf_h[:, :, 0:8].bitcast(F32), ALU.subtract)\
            .then_inc(S.wf_ready, 1)

    def ff_pool(pool, l, w):
        q = norm_index(l, 2 * w)
        f = 2 * l + w
        v0, v1 = K.evic(l, ("ff1in", "ff2in")[w]), K.evic(l, ("ff1out", "ff2out")[w])
        if w == 0:
            forget_pool(pool, l)
        with pool.Fori(0, FT) as i:
            n = FT * f + i
            pool.wait_ge(S.silu_ready, n + 1 + CREDIT)
            pool.wait_ge(S.evac, v0 + 2 * i + 4)
            pool.wait_ge(S.hid_ready, n + CREDIT)
            nc.gpsimd.tensor_tensor(K.g[:, :], K.silu[:, :], K.t2[:, :], ALU.mult).then_inc(S.g_ready, 1)
        pool_square(pool, q + 1, 0, v1, first=True)
        with pool.Fori(1, 8) as m:
            pool_square(pool, q + 1, m, v1 + m)

    def mix_pe(pe, l):
        q = norm_index(l, 1)
        pe.wait_ge(S.wf_ready, l + 1 + CREDIT)
        for k in range(8):
            pe.wait_ge(S.xg_ready, 8 * q + k + 1)
            for n, (a, b) in enumerate(((K.wf_h, xgh), (K.wf_h, xgl), (K.wf_l, xgh))):
                last = nc.tensor.matmul(pb[2][:, :], a[:, k, :], b[:, k, :],
                                        start=(k == 0 and n == 0), stop=(k == 7 and n == 2))
        last.then_inc(S.fl_ready, 1)
        s0, v0 = K.slab(l, "c"), K.evic(l, "c")
        pe_project(pe, s0, v0, 0)
        pe_sum_squares(pe, q)
        pe_project(pe, s0 + 1, v0 + 1, 1)
        with pe.Fori(1, 4) as i:
            for slot in range(2):
                pe_project(pe, s0 + 2 * i + slot, v0 + 2 * i + slot, slot)

        s1, v1 = K.slab(l, "at"), K.evic(l, "at")
        with pe.Fori(0, 4) as p:
            s, v = s1 + 6 * p, v1 + 6 * p
            pr = 4 * l + p
            for n in range(3):
                pe_project(pe, s + n, v + n, n % 2)

            def gate_part(n, lo, hi):
                slot = n % 2
                if lo == 0:
                    pe.wait_ge(S.raw_read, s + n + 1 + CREDIT)
                    pe.wait_ge(S.evac, v + n + 1)
                for k in range(lo, hi):
                    last = mm3(pb[slot][:, :], slot, k, xgh[:, k, :], xgl[:, k, :], k == 0, k == 7)
                if hi == 8:
                    last.then_inc(S.slab_done, 1)

            def forget(j):
                pe.wait_ge(S.cm_ready, 2 * pr + j + 1)
                if j == 0:
                    pe.wait_ge(S.vtok_ready, pr + CREDIT)
                else:
                    pe.wait_ge(S.cb_ready, 2 * pr + j)
                nc.tensor.matmul(pb[2][:, :], K.ones[0:8, :], K.cm[0:8, :], start=True, stop=True)\
                    .then_inc(S.cbp_ready, 1)

            def values():
                pe.wait_ge(S.evac, v + 5)
                pe.wait_ge(S.cb_ready, 2 * pr + 2)
                for t in range(4):
                    last = nc.tensor.transpose(pb[2][:, 128 * t:128 * t + 128], K.vt[:, 128 * t:128 * t + 128], K.ident[:, :])
                last.then_inc(S.vt_ready, 1)

            def scores(n):
                j, i = n // 4, n % 4
                pe.wait_ge(S.evac, v + 4)
                pe.wait_ge(S.neg_ready, 8 * pr + n - 1 + NEG_CREDIT)
                w = 128 * (i + 1)
                bank = pb[3 + n % 2]
                nc.tensor.matmul(bank[:, 0:w], K.qt[64 * j:64 * j + 64, 128 * i:128 * i + 128],
                                 K.kt[64 * j:64 * j + 64, 0:w], start=True, stop=False)
                nc.tensor.matmul(bank[:, w - 128:w], K.ident[:, :], K.future[:, :], start=False, stop=True)\
                    .then_inc(S.sc_ready, 1)

            def turn(n):
                i = n % 4
                pe.wait_ge(S.pn_ready, 8 * pr + n + 1)
                pe.wait_ge(S.ptc_ready, 8 * pr + n - 1 + CREDIT)
                for kk in range(i + 1):
                    last = nc.tensor.transpose(pb[5 + n % 2][:, 128 * kk:128 * kk + 128],
                                               K.pr[n % 2][:, 128 * kk:128 * kk + 128], K.ident[:, :])
                last.then_inc(S.ptp_ready, 1)

            def attend(j):
                pe.wait_ge(S.ptc_ready, 8 * pr + 4 * j + 4 + CREDIT)
                if j == 0:
                    pe.wait_ge(S.vtok_ready, pr + 1 + CREDIT)
                    pe.wait_ge(S.ao_ready, pr + CREDIT)
                for kk in range(4):
                    last = nc.tensor.matmul(pb[7][64 * j:64 * j + 64, 128 * kk:512],
                                            K.vtok[:, kk, 64 * j:64 * j + 64], K.pt[:, kk, 128 * kk:512],
                                            start=(kk == 0), stop=(kk == 3))
                last.then_inc(S.at_ready, 1)

            forget(0)
            forget(1)
            scores(0)
            scores(1)
            gate_part(3, 0, 4)
            values()
            turn(0)
            scores(2)
            gate_part(3, 4, 8)
            turn(1)
            scores(3)
            gate_part(4, 0, 2)
            turn(2)
            scores(4)
            gate_part(4, 2, 4)
            turn(3)
            scores(5)
            gate_part(4, 4, 6)
            attend(0)
            turn(4)
            scores(6)
            gate_part(4, 6, 8)
            turn(5)
            scores(7)
            gate_part(5, 0, 3)
            turn(6)
            gate_part(5, 3, 6)
            turn(7)
            gate_part(5, 6, 8)
            attend(1)

        s2, v2 = K.slab(l, "gr"), K.evic(l, "gr")
        for n in range(4):
            if n == 2:
                pe.wait_ge(S.ao_ready, 4 * (l + 1) + CREDIT)
                pe.wait_ge(S.sq_added2, 4 * (l + 1))
                nc.tensor.matmul(pb[7][:, :], K.ones[:, :], K.sqsum[:, :], start=True, stop=True).then_inc(S.css_ready, 1)
            pe_project(pe, s2 + n, v2 + n, n % 2)

        s3, v3 = K.slab(l, "am"), K.evic(l, "am")
        pe.wait_ge(S.ao_ready, 4 * (l + 1) + CREDIT)

        def am(m, slot, first):
            pe.wait_ge(S.raw_read, s3 + m + 1 + CREDIT)
            pe.wait_ge(S.evac, v3 + m + 1)
            for k in range(4):
                mm3(pb[slot][:, :], slot, k, K.ao_h[:, k, :], K.ao_l[:, k, :], k == 0, k == 3)
            if first:
                pe.wait_ge(S.cv_ready, 4 * (l + 1))
            for k in range(4):
                last = mm3(pb[2 + slot][:, :], slot, 4 + k, K.cv_h[:, k, :], K.cv_l[:, k, :], k == 0, k == 3)
            last.then_inc(S.slab_done, 1)
        am(0, 0, True)
        am(1, 1, False)
        with pe.Fori(1, 4) as i:
            for slot in range(2):
                am(2 * i + slot, slot, False)

        s4, v4 = K.slab(l, "wo"), K.evic(l, "wo")

        def wo(m, slot, first):
            pe.wait_ge(S.raw_read, s4 + m + 1 + CREDIT)
            pe.wait_ge(S.evac, v4 + m + 1)
            for k in range(8):
                if first:
                    pe.wait_ge(S.mg_ready, 8 * l + k + 1)
                last = mm3(pb[slot][:, :], slot, k, K.mg_h[:, k, :], K.mg_l[:, k, :], k == 0, k == 7)
            last.then_inc(S.slab_done, 1)
        wo(0, 0, True)
        wo(1, 1, False)
        with pe.Fori(1, 4) as i:
            for slot in range(2):
                wo(2 * i + slot, slot, False)

    def mix_act(act, l):
        q = norm_index(l, 1)
        s0, v0 = K.slab(l, "c"), K.evic(l, "c")

        def glu(i, first):
            split_hi(act, s0 + 2 * i + 2, 0, 1024)
            if first:
                act_std(act, q)
            split_hi(act, s0 + 2 * i + 3, 1, 1024)
            act.wait_ge(S.evac, v0 + 2 * i + 4)
            act.wait_ge(S.glu_ready, 4 * l + i + CREDIT)
            nc.scalar.activation(K.silu[:, :], K.t2[:, :], ACT.Sigmoid).then_inc(S.glus_ready, 1)
        glu(0, True)
        with act.Fori(1, 4) as i:
            glu(i, False)
        act.wait_ge(S.fa_ready, l + 1)
        nc.scalar.activation(K.fe[0:8, :], K.fe[0:8, :], ACT.Exp, scale=-1.0).then_inc(S.fe_ready, 1)
        act.wait_ge(S.fe_ready, l + 1)
        nc.scalar.activation(K.fe[0:8, :], K.fe[0:8, :], ACT.Ln, bias=1.0).then_inc(S.fln_ready, 1)

        s1, v1 = K.slab(l, "at"), K.evic(l, "at")
        with act.Fori(0, 4) as p:
            s, v = s1 + 6 * p, v1 + 6 * p
            pr = 4 * l + p
            split_hi(act, s + 2, 0, 1024)
            split_hi(act, s + 3, 1, 1024)
            split_hi(act, s + 4, 0, 1024)

            def cb(j):
                act.wait_ge(S.cbp_ready, 2 * pr + j + 1 + CREDIT)
                act.wait_ge(S.neg_ready, 8 * pr + 4 * j - 4 + NEG_CREDIT)
                nc.scalar.activation(K.cb[j][:, :], pb[2][:, :], ACT.Copy).then_inc(S.cb_ready, 1)
            cb(0)
            cb(1)

            def exp(n):
                w = 128 * (n % 4 + 1)
                act.wait_ge(S.neg_ready, 8 * pr + n + 1 + NEG_CREDIT)
                act.wait_ge(S.ptp_ready, 8 * pr + n - 1 + CREDIT)
                nc.scalar.activation(K.pr[n % 2][:, 0:w], K.lg[n % 2][:, 0:w], ACT.Exp, scale=-1.0,
                                     bias=K.negmax[:, n:n + 1], accum_out=K.rowsum[:, n:n + 1]).then_inc(S.pe_ready, 1)

            def pcopy(n):
                i = n % 4
                act.wait_ge(S.ptp_ready, 8 * pr + n + 1 + CREDIT)
                if i == 0:
                    act.wait_ge(S.at_ready, 2 * pr + n // 4 + CREDIT)
                nc.scalar.activation(K.pt[:, 0:i + 1, 128 * i:128 * i + 128],
                                     pb[5 + n % 2][:, 0:128 * (i + 1)].rearrange("p (k c) -> p k c", c=128),
                                     ACT.Copy).then_inc(S.ptc_ready, 1)
            exp(0)
            act.wait_ge(S.vt_ready, pr + 1)
            act.wait_ge(S.at_ready, 2 * pr + CREDIT)
            nc.scalar.activation(K.vtok[:, :, :], pb[2][:, :].rearrange("p (t c) -> p t c", c=128), ACT.Copy)\
                .then_inc(S.vtok_ready, 1)
            exp(1)
            split_hi(act, s + 5, 1, 1024)
            pcopy(0)
            exp(2)
            pcopy(1)
            exp(3)
            pcopy(2)
            exp(4)
            pcopy(3)
            exp(5)
            pcopy(4)
            split_hi(act, s + 6, 0, 1024)
            exp(6)
            pcopy(5)
            exp(7)
            pcopy(6)
            pcopy(7)
            split_hi(act, s + 7, 1, 1024)
            act.wait_ge(S.at_ready, 2 * pr + 2 + CREDIT)
            nc.scalar.activation(K.ao_h[:, p, :], pb[7][:, :], ACT.Copy).then_inc(S.aoh_ready, 1)

        s2, v2 = K.slab(l, "gr"), K.evic(l, "gr")
        split_hi(act, s2 + 2, 0, 1024)
        split_hi(act, s2 + 3, 1, 1024)
        act.wait_ge(S.css_ready, l + 1)
        act.wait_ge(S.rstd_ready, q + 1 + CREDIT)
        nc.scalar.activation(K.std[:, :], pb[7][:, :], ACT.Sqrt, bias=K.eps[:, 0:1], scale=1.0 / 512)\
            .then_inc(S.cstd_ready, 1)
        split_hi(act, s2 + 4, 0, 1024)
        for t in range(4):
            act.wait_ge(S.cn_ready, 4 * l + t + 1)
            nc.scalar.activation(K.cy[:, t, :], K.cy[:, t, :], ACT.Silu).then_inc(S.cs_ready, 1)
        split_hi(act, s2 + 5, 1, 1024)
        for t in range(4):
            act.wait_ge(S.cs_ready, 4 * l + t + 1)
            nc.scalar.activation(K.cv_h[:, t, :], K.cy[:, t, :], ACT.Copy).then_inc(S.cvh_ready, 1)

        s3, v3 = K.slab(l, "am"), K.evic(l, "am")

        def sigmoids(m, slot):
            act.wait_ge(S.merged, 8 * l + m - 1 + CREDIT)
            nc.scalar.activation(K.sig[slot][0][:, :], K.gates[:, m, :], ACT.Sigmoid).then_inc(S.sa_ready, 1)
            nc.scalar.activation(K.sig[slot][1][:, :], K.gates[:, 8 + m, :], ACT.Sigmoid).then_inc(S.sa_ready, 1)

        def am(m, slot, last=False):
            if not last:
                sigmoids(m + 1, 1 - slot)
            split_hi(act, s3 + m + 2, slot, 1024)
            act.wait_ge(S.merged, 8 * l + m + 1 + CREDIT)
            hold(act, S)
            nc.scalar.activation(K.mg_h[:, m, :], K.g[:, :], ACT.Copy).then_inc(S.mgh_ready, 1)
        act.wait_ge(S.evac, v3 + 2)
        sigmoids(0, 0)
        with act.Fori(0, 3) as i:
            for slot in range(2):
                am(2 * i + slot, slot)
        am(6, 0)
        am(7, 1, True)
        s4, v4 = K.slab(l, "wo"), K.evic(l, "wo")
        with act.Fori(0, 4) as i:
            for slot in range(2):
                m = 2 * i + slot
                act_gain(act, q + 1, m, v4 + m)
                split_hi(act, s4 + m + 2, slot, 1024)

    def mix_dve(dve, l):
        q = norm_index(l, 1)
        s0, v0 = K.slab(l, "c"), K.evic(l, "c")

        dve.wait_ge(S.edge_zero, l + 1)

        def glu(i, first):
            split_lo(dve, s0 + 2 * i + 2, 0, 1024)
            if first:
                dve_rstd(dve, q, v0)
            nc.vector.tensor_tensor(K.glu[:, i, 30:542], pb[0][:, :], rstd[:, :], ALU.mult).then_inc(S.evac, 1)
            split_lo(dve, s0 + 2 * i + 3, 1, 1024)
            nc.vector.tensor_tensor(K.t2[:, :], pb[1][:, :], rstd[:, :], ALU.mult).then_inc(S.evac, 1)
            dve.wait_ge(S.glus_ready, 4 * l + i + 1)
            nc.vector.tensor_tensor(K.glu[:, i, 30:542], K.glu[:, i, 30:542], K.silu[:, :], ALU.mult)\
                .then_inc(S.glu_ready, 1)
            dve.wait_ge(S.glu_ready, 4 * l + i + 1 + CREDIT)
        glu(0, True)
        R = slice(0, 8)
        chain = K.fchain
        chain.enter(l, FCHAIN)
        dve.wait_ge(S.fl_ready, l + 1)
        chain.link(nc.vector.tensor_tensor(K.fx[R, :], pb[2][R, :], rstd[R, :], ALU.mult))
        chain.link(nc.vector.tensor_scalar(K.fx[R, :], K.fx[R, :], K.bf[R, bass.ds(l, 1)], None, ALU.add))
        chain.link(nc.vector.tensor_scalar(K.fc[R, :], K.fx[R, :], -1.0, None, ALU.mult))
        nc.vector.tensor_tensor(K.fe[R, :], K.fx[R, :], K.fc[R, :], ALU.max).then_inc(S.fa_ready, 1)
        chain.link(nc.vector.tensor_scalar(K.fx[R, :], K.fx[R, :], 0.0, None, ALU.min))
        chain.link(nc.vector.memset(K.onerow[R, :], 1.0))
        hold(dve, S)
        with dve.Fori(1, 4) as i:
            glu(i, False)
        dve.wait_ge(S.fln_ready, l + 1)
        chain.link(nc.vector.tensor_tensor(K.fx[R, :], K.fx[R, :], K.fe[R, :], ALU.subtract))
        chain.link(nc.vector.tensor_tensor_scan(K.fc[R, :], K.onerow[R, :], K.fx[R, :], 0.0, ALU.mult, ALU.add))
        chain.leave(LAYERS, FCHAIN)
        hold(dve, S)

        s1, v1 = K.slab(l, "at"), K.evic(l, "at")
        tap = K.tapchain
        with dve.Fori(0, 4) as p:
            s, v = s1 + 6 * p, v1 + 6 * p
            pr = 4 * l + p
            tap.enter(pr, CONV_TAPS)

            def taps(lo, hi):
                for k in range(lo, hi):
                    wk = K.cw[:, bass.ds(4 * CONV_TAPS * l + CONV_TAPS * p + k, 1)]
                    if k == 0:
                        tap.link(nc.vector.tensor_scalar(K.cy[:, p, :], K.glu[:, p, 0:512], wk,
                                                         K.cbias[:, bass.ds(4 * l + p, 1)], ALU.mult, ALU.add))
                    else:
                        tap.link(nc.vector.scalar_tensor_tensor(out=K.cy[:, p, :], in0=K.glu[:, p, k:k + 512],
                                                                scalar=wk, in1=K.cy[:, p, :],
                                                                op0=ALU.mult, op1=ALU.add))

            def gate_out(n, slot):
                nc.vector.tensor_tensor(K.gates[:, 3 * p + n, :], pb[slot][:, :], rstd[:, :], ALU.mult)\
                    .then_inc(S.evac, 1)

            def cm(j):
                dve.wait_ge(S.cbp_ready, 2 * pr + j + CREDIT)
                nc.vector.tensor_scalar(K.cm[0:8, :], K.fc[0:8, :], K.ident[0:8, bass.ds(2 * p + j, 1)], None, ALU.mult)\
                    .then_inc(S.cm_ready, 1)

            def logits(n):
                w = 128 * (n % 4 + 1)
                dve.wait_ge(S.sc_ready, 8 * pr + n + 1)
                dve.wait_ge(S.cb_ready, 2 * pr + n // 4 + 1)
                dve.wait_ge(S.pe_ready, 8 * pr + n - 1 + CREDIT)
                hold(dve, S)
                nc.vector.tensor_tensor_reduce(K.lg[n % 2][:, 0:w], K.cb[n // 4][:, 0:w], pb[3 + n % 2][:, 0:w], 1.0, 3.0e38,
                                               ALU.add, ALU.min, K.negmax[:, n:n + 1]).then_inc(S.neg_ready, 1)

            def probs(n):
                w = 128 * (n % 4 + 1)
                dve.wait_ge(S.pe_ready, 8 * pr + n + 1 + CREDIT)
                nc.vector.reciprocal(K.rowinv[:, n:n + 1], K.rowsum[:, n:n + 1]).then_inc(S.ri_ready, 1)
                dve.wait_ge(S.ri_ready, 8 * pr + n + 1)
                nc.vector.tensor_scalar(K.pr[n % 2][:, 0:w], K.pr[n % 2][:, 0:w], K.rowinv[:, n:n + 1], None, ALU.mult)\
                    .then_inc(S.pn_ready, 1)

            cm(0)
            split_lo(dve, s + 2, 0, 1024)
            nc.vector.scalar_tensor_tensor(out=K.qt[:, :], in0=pb[0][:, :], scalar=-HEAD_DIM_2 ** -0.5, in1=rstd[:, :],
                                           op0=ALU.mult, op1=ALU.mult).then_inc(S.evac, 1)
            taps(0, 2)
            split_lo(dve, s + 3, 1, 1024)
            nc.vector.tensor_tensor(K.kt[:, :], pb[1][:, :], rstd[:, :], ALU.mult).then_inc(S.evac, 1)
            cm(1)
            taps(2, 4)
            split_lo(dve, s + 4, 0, 1024)
            dve.wait_ge(S.vtok_ready, pr + CREDIT)
            nc.vector.tensor_tensor(K.vt[:, :], pb[0][:, :], rstd[:, :], ALU.mult).then_inc(S.evac, 1)
            logits(0)
            logits(1)
            probs(0)
            taps(4, 6)
            logits(2)
            probs(1)
            split_lo(dve, s + 5, 1, 1024)
            gate_out(0, 1)
            taps(6, 8)
            logits(3)
            probs(2)
            taps(8, 11)
            logits(4)
            probs(3)
            taps(11, 14)
            logits(5)
            probs(4)
            taps(14, 17)
            split_lo(dve, s + 6, 0, 1024)
            gate_out(1, 0)
            logits(6)
            probs(5)
            taps(17, 20)
            logits(7)
            probs(6)
            taps(20, 23)
            probs(7)
            taps(23, 28)
            split_lo(dve, s + 7, 1, 1024)
            gate_out(2, 1)
            dve.wait_ge(S.aoh_ready, pr + 1)
            nc.vector.tensor_tensor(K.ao_l[:, p, :], pb[7][:, :], K.ao_h[:, p, :].bitcast(F32), ALU.subtract)\
                .then_inc(S.ao_ready, 1)
            taps(28, CONV_TAPS)
            tap.leave(4 * LAYERS, CONV_TAPS)

        s2, v2 = K.slab(l, "gr"), K.evic(l, "gr")

        def late_gate(n):
            split_lo(dve, s2 + n + 2, n % 2, 1024)
            nc.vector.tensor_tensor(K.gates[:, 12 + n, :], pb[n % 2][:, :], rstd[:, :], ALU.mult).then_inc(S.evac, 1)
        late_gate(0)
        late_gate(1)
        dve.wait_ge(S.cstd_ready, l + 1)
        nc.vector.reciprocal(K.crstd[:, :], K.std[:, :]).then_inc(S.crstd_ready, 1)
        dve.wait_ge(S.crstd_ready, l + 1)
        for t in range(4):
            nc.vector.scalar_tensor_tensor(out=K.cy[:, t, :], in0=K.cy[:, t, :], scalar=K.gconv[:, bass.ds(4 * l + t, 1)],
                                           in1=K.crstd[:, :], op0=ALU.mult, op1=ALU.mult).then_inc(S.cn_ready, 1)
        late_gate(2)
        late_gate(3)
        for t in range(4):
            dve.wait_ge(S.cvh_ready, 4 * l + t + 1)
            nc.vector.tensor_tensor(K.cv_l[:, t, :], K.cy[:, t, :], K.cv_h[:, t, :].bitcast(F32), ALU.subtract)\
                .then_inc(S.cv_ready, 1)

        s3, v3 = K.slab(l, "am"), K.evic(l, "am")

        def merged_low(m):
            dve.wait_ge(S.mgh_ready, 8 * l + m + 1)
            nc.vector.tensor_tensor(K.mg_l[:, m, :], K.g[:, :], K.mg_h[:, m, :].bitcast(F32), ALU.subtract)\
                .then_inc(S.mg_ready, 1)
            dve.wait_ge(S.mg_ready, 8 * l + m + 1)

        def am(m, slot, first=False):
            if not first:
                merged_low(m - 1)
            split_lo(dve, s3 + m + 2, slot, 1024)
            dve.wait_ge(S.sa_ready, 16 * l + 2 * m + 2)
            nc.vector.tensor_tensor(K.ma[:, :], K.sig[slot][0][:, :], pb[slot][:, :], ALU.mult).then_inc(S.ma_ready, 1)
            nc.vector.tensor_tensor(K.mc[:, :], K.sig[slot][1][:, :], pb[2 + slot][:, :], ALU.mult).then_inc(S.evac, 1)
            dve.wait_ge(S.ma_ready, 8 * l + m + 1)
            dve.wait_ge(S.evac, v3 + m + 3)
            nc.vector.tensor_tensor(K.g[:, :], K.ma[:, :], K.mc[:, :], ALU.add).then_inc(S.merged, 1)
        am(0, 0, True)
        am(1, 1)
        with dve.Fori(1, 4) as i:
            for slot in range(2):
                am(2 * i + slot, slot)
        merged_low(7)
        hold(dve, S)
        s4, v4 = K.slab(l, "wo"), K.evic(l, "wo")
        with dve.Fori(0, 4) as i:
            for slot in range(2):
                m = 2 * i + slot
                dve.wait_ge(S.slab_done, s4 + m + 1 + CREDIT)
                nc.vector.tensor_tensor(h[:, m, :], pb[slot][:, :], h[:, m, :], ALU.add).then_inc(S.evac, 1)
                dve_gain(dve, q + 1, m)
                split_lo(dve, s4 + m + 2, slot, 1024)

    def mix_pool(pool, l):
        q = norm_index(l, 1)
        pool.wait_ge(S.slab_done, K.slab(l, "c") + 2)
        hold(pool, S)
        nc.gpsimd.memset(K.glu[:, :, 0:CONV_TAPS - 1], 0.0).then_inc(S.edge_zero, 1)
        pool.wait_ge(S.ss_ready, q + 1)
        hold(pool, S)
        nc.gpsimd.memset(K.sqsum[:, :], 0.0).then_inc(S.sq_zeroed2, 1)
        pool.wait_ge(S.sq_zeroed2, l + 1)
        hold(pool, S)
        with pool.Fori(0, 4) as p:
            n = 4 * l + p
            pool.wait_ge(S.tap_done, CONV_TAPS * (n + 1))
            nc.gpsimd.tensor_tensor(K.sqtmp[:, :], K.cy[:, p, :], K.cy[:, p, :], ALU.mult).then_inc(S.sq_made2, 1)
            pool.wait_ge(S.sq_made2, n + 1)
            nc.gpsimd.tensor_tensor(K.sqsum[:, :], K.sqsum[:, :], K.sqtmp[:, :], ALU.add).then_inc(S.sq_added2, 1)
            pool.wait_ge(S.sq_added2, n + 1)
        v4 = K.evic(l, "wo")
        pool.wait_ge(S.css_ready, l + 1)
        pool_square(pool, q + 1, 0, v4, first=True)
        with pool.Fori(1, 8) as m:
            pool_square(pool, q + 1, m, v4 + m)

    def ple_pe(pe, l):
        q = norm_index(l, 3)
        s0, v0 = K.slab(l, "ple"), K.evic(l, "ple")

        def tile(m, slot, first):
            pe.wait_ge(S.raw_read, s0 + m + 1 + CREDIT)
            pe.wait_ge(S.evac, v0 + m + 1)
            if first:
                pe.wait_ge(S.pl_ready, l + 1)
            for k in range(2):
                mm3(pb[2 + slot][:, :], slot, 8 + k, K.p_h[:, k, :], K.p_l[:, k, :], k == 0, k == 1)
            for k in range(8):
                if first:
                    pe.wait_ge(S.xg_ready, 8 * q + k + 1)
                last = mm3(pb[slot][:, :], slot, k, xgh[:, k, :], xgl[:, k, :], k == 0, k == 7)
            last.then_inc(S.slab_done, 1)
        tile(0, 0, True)
        pe_sum_squares(pe, q)
        tile(1, 1, False)
        with pe.Fori(1, 4) as i:
            for slot in range(2):
                tile(2 * i + slot, slot, False)

    def embed_act(act, l):
        act.wait_ge(S.p_raw, 16 * (l + 1))
        nc.scalar.activation(K.p_h[:, :, :], K.p_in[:, :, :], ACT.Copy).then_inc(S.ph_ready, 1)

    def embed_dve(dve, l):
        dve.wait_ge(S.ph_ready, l + 1)
        nc.vector.tensor_tensor(K.p_l[:, :, :], K.p_in[:, :, :], K.p_h[:, :, :].bitcast(F32), ALU.subtract)\
            .then_inc(S.pl_ready, 1)

    def ple_act(act, l):
        q = norm_index(l, 3)
        s0, v0 = K.slab(l, "ple"), K.evic(l, "ple")

        def tile(m, slot, first, cols=1280):
            if cols:
                split_hi(act, s0 + m + 2, slot, cols)
            if first:
                act_std(act, q)
            act.wait_ge(S.gt_ready, 8 * l + m + 1)
            nc.scalar.activation(K.silu[:, :], K.t1[:, :], ACT.Sigmoid).then_inc(S.gs_ready, 1)
        tile(0, 0, True)
        tile(1, 1, False)
        with act.Fori(1, 3) as i:
            for slot in range(2):
                tile(2 * i + slot, slot, False)
        tile(6, 0, False, 1024)
        tile(7, 1, False, 1024)
        with act.Fori(0, 8) as m:
            act_gain(act, q + 1, m, v0 + m)

    def ple_dve(dve, l):
        q = norm_index(l, 3)
        s0, v0 = K.slab(l, "ple"), K.evic(l, "ple")

        def tile(m, slot, first, cols=1280):
            split_lo(dve, s0 + m + 2, slot, cols)
            if first:
                dve_rstd(dve, q, v0)
            n = 8 * l + m
            dve.wait_ge(S.gu_ready, n + CREDIT)
            nc.vector.tensor_tensor(K.t1[:, :], pb[slot][:, :], rstd[:, :], ALU.mult).then_inc(S.gt_ready, 1)
            dve.wait_ge(S.gs_ready, n + 1)
            nc.vector.tensor_tensor(K.t2[:, :], K.silu[:, :], pb[2 + slot][:, :], ALU.mult).then_inc(S.gu_ready, 1)
            dve.wait_ge(S.gu_ready, n + 1 + CREDIT)
            nc.vector.tensor_tensor(h[:, m, :], K.t2[:, :], h[:, m, :], ALU.add).then_inc(S.evac, 1)
        tile(0, 0, True)
        tile(1, 1, False)
        with dve.Fori(1, 3) as i:
            for slot in range(2):
                tile(2 * i + slot, slot, False)
        tile(6, 0, False, 1024)
        tile(7, 1, False, 1024)
        with dve.Fori(0, 8) as m:
            dve_gain(dve, q + 1, m)

    def ple_pool(pool, l):
        q = norm_index(l, 3)
        v0 = K.evic(l, "ple")
        pool_square(pool, q + 1, 0, v0, first=True)
        with pool.Fori(1, 8) as m:
            pool_square(pool, q + 1, m, v0 + m)

    def pe_prog(pe):
        with pe.Fori(0, LAYERS) as l:
            ff_pe(pe, l, 0)
            mix_pe(pe, l)
            ff_pe(pe, l, 1)
            ple_pe(pe, l)
        pe_sum_squares(pe, 4 * LAYERS)

    def act_prog(act):
        with act.Fori(0, LAYERS) as l:
            ff_act(act, l, 0)
            mix_act(act, l)
            ff_act(act, l, 1)
            ple_act(act, l)
        act_std(act, 4 * LAYERS)

    def dve_prog(dve):
        with dve.Fori(0, LAYERS) as l:
            ff_dve(dve, l, 0)
            mix_dve(dve, l)
            ff_dve(dve, l, 1)
            ple_dve(dve, l)
        dve_rstd(dve, 4 * LAYERS, K.evic(LAYERS, "ff1in"))
        for m in range(8):
            nc.vector.scalar_tensor_tensor(out=K.outt[:, m, :], in0=h[:, m, :],
                                           scalar=K.gains[:, 32 * LAYERS + m:32 * LAYERS + m + 1],
                                           in1=rstd[:, :], op0=ALU.mult, op1=ALU.mult).then_inc(S.out_ready, 1)

    def pool_prog(pool):
        with pool.Fori(0, LAYERS) as l:
            ff_pool(pool, l, 0)
            mix_pool(pool, l)
            ff_pool(pool, l, 1)
            ple_pool(pool, l)

    def sp_prog(sp):
        with sp.Fori(0, LAYERS) as l:
            K.stream(sp, K.slab(l, "ff1in"), K.w_ff1in, 2 * FT, l, 1024)
            sp.wait_ge(S.wf_ready, l + CREDIT)
            sp.dma_start(K.wf[:, :, :], K.w_f[l, :, :].rearrange("p (k c) -> p k c", c=8)).then_inc(S.wf_raw, 16)
            K.stream(sp, K.slab(l, "ff1out"), K.w_ff1out, 16, l, 1408)
            K.stream(sp, K.slab(l, "c"), K.w_mix, 36, l, 1024)
            K.stream(sp, K.slab(l, "am"), K.w_am, 8, l, 1024)
            K.stream(sp, K.slab(l, "wo"), K.w_wo, 8, l, 1024)
            K.stream(sp, K.slab(l, "ff2in"), K.w_ff2in, 2 * FT, l, 1024)
            sp.wait_ge(S.cb_ready, 8 * (l + 1))
            sp.wait_ge(S.slab_done, K.slab(l, "ff2in") + 2)
            sp.dma_start(K.p_in[:, :, :], K.p_t[l, :, :].rearrange("p (k c) -> p k c", c=512)).then_inc(S.p_raw, 16)
            K.stream(sp, K.slab(l, "ff2out"), K.w_ff2out, 16, l, 1408)
            K.stream(sp, K.slab(l, "ple"), K.w_ple, 8, l, 1280)
        K.stream(sp, K.slab(LAYERS, "ff1in"), K.w_ff1in, 2, 0, 1024)
        with sp.Fori(0, 8) as m:
            sp.wait_ge(S.out_ready, m + 1)
            sp.dma_start(K.out[m, :, :], K.outt[:, m, :]).then_inc(S.out_done, 16)
        sp.wait_ge(S.out_done, 16 * 8)

    return sp_prog, act_prog, dve_prog, pe_prog, pool_prog


def first_arrays(A):
    r = {}
    r["x_t"] = A["x"][0].T.reshape(8, 128, TOK).transpose(1, 0, 2)
    r["ctx_t"] = A["ctx"][0].T.reshape(8, 128, CTX).transpose(1, 0, 2)
    r["cond"] = np.stack([A["c"][0], A["c_ctx"]]).reshape(2, 8, 128).transpose(2, 1, 0)
    r["b_mod"] = columns(A["b_mod"])
    r["n_gain"] = columns(A["norm_gain"])
    r["dn_gain"] = columns(A["dn_norm_gain"])
    r["p_scale"] = columns(A["pool_scale"])
    r["f_gain"] = columns(A["final_gain"][None])
    r["a_log"] = np.broadcast_to(A["a_log"].reshape(1, 16), (128, 16))
    r["dt_bias"] = np.broadcast_to(A["dt_bias"].reshape(1, 16), (128, 16))
    r["short_w"] = A["conv_w"][0].reshape(SHORT, 24, 128).transpose(2, 1, 0).reshape(128, -1)
    r["w_mod"] = tape(A["w_mod"][0])
    w_in = A["w_in"][0]
    order = [kind * 8 + 2 * g + j for g in range(GROUPS) for kind, j in HEAD_SLABS]
    r["w_dn"] = tape(w_in[:, 0:3072], order)
    r["w_ab"] = w_in[:, 3072:3104].reshape(8, 128, 32).transpose(1, 0, 2)
    z_dn, u_pool, z_pool = (tape(w_in[:, a:a + 1024]) for a in (3104, 4128, 5152))
    pool_w = A["pool_w"][0].reshape(2, 2, 2, 128, 2, 128).transpose(0, 3, 1, 4, 2, 5).reshape(2, 1, 128, 1024)
    r["w_tail"] = np.stack([{"u": u_pool, "z": z_dn, "w": pool_w[:, 0], "p": z_pool}[kind][m] for kind, m in TAIL])
    t = A["w_out"][0].reshape(16, 128, 8, 128)[list(OUT_ORDER)]
    r["w_out1"] = t.reshape(2, 8, 128, 8, 128).transpose(3, 0, 2, 1, 4).reshape(16, 128, 1024)
    return {k: np.ascontiguousarray(v) for k, v in r.items()}


def first_const_arrays():
    s, c = np.arange(128)[:, None], np.arange(128)[None, :]
    same = s // CHUNK == c // CHUNK
    level = np.zeros((LEVELS, 128, 2, 128), np.float32)
    for l in range(LEVELS):
        block = s // (2 << l) == c // (2 << l)
        first = lambda a: a // (1 << l) % 2 == 0
        level[l, :, 0] = block & first(s) & ~first(c)
        level[l, :, 1] = block & first(c) & ~first(s)
    incl = np.stack([same & (s <= c), same & (s >= c)])
    y, x = np.arange(GRID_H), np.arange(GRID_W)
    counts = []
    for w in WINDOWS:
        span = lambda a, n: np.clip(a - w // 2 + w, 0, n) - np.clip(a - w // 2, 0, n)
        counts.append((span(y, GRID_H)[:, None] * span(x, GRID_W)[None, :]).reshape(1, TOK))
    icnt = np.broadcast_to(1.0 / np.stack(counts), (len(WINDOWS), 128, TOK))
    r = {"c_level": level, "c_incl": incl, "c_icnt": icnt,
         "c_epsq": np.full((128, 1), 128 * EPS)}
    return {k: np.ascontiguousarray(v, dtype=np.float32) for k, v in r.items()}


def build_program(nc, a):
    with ExitStack() as ctx:
        S = make_sems(nc, ctx)
        K = Names()
        K.S, K.nc, K.out, K.c_icnt = S, nc, a["out"], a["c_icnt"]
        K.w_mod, K.w_dn, K.w_tail, K.w_out1 = a["w_mod"], a["w_dn"], a["w_tail"], a["w_out1"]
        K.w_ff1in, K.w_ff1out, K.w_ff2in, K.w_ff2out = a["w_ff1in"], a["w_ff1out"], a["w_ff2in"], a["w_ff2out"]
        K.w_mix, K.w_am, K.w_wo, K.w_ple, K.w_f, K.p_t = a["w_mix"], a["w_am"], a["w_wo"], a["w_ple"], a["w_f"], a["p_t"]
        make_common(nc, K, LAYER_SLAB, LAYER_EVIC, MOD_SLABS)
        at = make_shared_memory(nc, K, ctx)
        make_layer_memory(nc, K, at)
        make_first_memory(nc, K, at)
        K.cond = a["cond"]
        consts = [(K.eps[:, :], a["c_eps"]), (K.epsq[:, :], a["c_epsq"]),
                       (K.bmod[:, :], a["b_mod"]), (K.ngain[:, :], a["n_gain"]), (K.ones[:, :], a["c_ones"]),
                       (K.ident[:, :], a["c_ident"]), (K.incl[0][:, :], a["c_incl"][0, :, :]),
                       (K.incl[1][:, :], a["c_incl"][1, :, :]),
                       (K.wk[:, :], a["short_w"]), (K.dngain[:, :], a["dn_gain"]), (K.pscale[:, :], a["p_scale"]),
                       (K.fgain[:, :], a["f_gain"]), (K.gains[:, :], a["gains"]), (K.cw[:, :], a["cw"]),
                       (K.cbias[:, :], a["cbias"]), (K.gconv[:, :], a["gconv"]), (K.bf[:, :], a["bf"]),
                       (K.future[:, :], a["c_future"])]
        consts += [(K.level[l][:, :, :], a["c_level"][l, :, :, :]) for l in range(LEVELS)]
        K.consts_act = [(K.h[:, :, :], a["x_t"]), (K.ctx[:, :, :], a["ctx_t"]), (K.wab[:, :, :], a["w_ab"]),
                        (K.alog[:, :], a["a_log"]), (K.dtb[:, :], a["dt_bias"])] + consts
        sp2, act2, dve2, pe2, pool2 = transformer_layers(K)
        sp1, act1, dve1, pe1, pool1 = delta_block(K)
        block = ctx.enter_context(nc.Block())

        @block.sync
        def _(sp):
            sp1(sp)
            sp2(sp)

        @block.scalar
        def _(act):
            act1(act)
            act2(act)

        @block.vector
        def _(dve):
            K.fchain = Chain(dve, S.forget_step)
            K.tapchain = Chain(dve, S.tap_done)
            dve1(dve)
            dve2(dve)

        @block.tensor
        def _(pe):
            pe1(pe)
            pe2(pe)

        @block.gpsimd
        def _(pool):
            start_credits(pool, S)
            pool1(pool)
            pool2(pool)


def kernel(**inputs):
    import concourse.bacc as bacc
    from concourse.bass_utils import run_bass_kernel_spmd

    given = {n: np.asarray(v) for n, v in inputs.items()}
    arrays = {**first_arrays(given), **first_const_arrays(), **layer_arrays(given), **const_arrays()}
    nc = bacc.Bacc("TRN2", target_bir_lowering=False, num_devices=1)
    args = {n: nc.dram_tensor(n, v.shape, mybir.dt.from_np(v.dtype), kind="ExternalInput").ap()
            for n, v in arrays.items()}
    args["out"] = nc.dram_tensor("out", (8, 128, TOK), F32, kind="ExternalOutput").ap()
    build_program(nc, args)
    r = run_bass_kernel_spmd(nc, [arrays], core_ids=[0])
    return np.ascontiguousarray(r.results[0]["out"].reshape(D, TOK).T).reshape(1, TOK, D)
```
